# Optimizing a Trainium2 kernel written in Bass

```python
import math
import jax, jax.numpy as jnp
from jax import lax
import numpy as np

D_MODEL = 1024
BATCH = 1
SEQ = 1024
DEPTH = 1

GRID_W = 64
CTX_LEN = 256
ATTN_WIDTH = 512
HYENA_WIDTH = 512
MIX_WIDTH = ATTN_WIDTH + HYENA_WIDTH
HEAD_DIM = 64
N_Q_HEADS = ATTN_WIDTH // HEAD_DIM
N_KV_HEADS = 2
Q_PER_KV = N_Q_HEADS // N_KV_HEADS
KV_WIDTH = N_KV_HEADS * HEAD_DIM
HYENA_GROUPS = 8
IN_WIDTH = ATTN_WIDTH + 2 * KV_WIDTH + 3 * HYENA_WIDTH
SHORT_CONV = 3
FILTER_EMB = 33
FILTER_ORDER = 64
DECAY_TARGET = 1e-2
FAST_DECAY_PCT = 0.3
SLOW_DECAY_PCT = 1.5
N_EXPERTS = 16
CAPACITY_FACTOR = 2
D_EXPERT = 2752
ROPE_THETA = 10000.0
Q_BLOCK = 128
EPS = 1e-6

kernel_name = "hybrid_hyena_gqa_ec_moe_dit_layer"

F32 = jnp.float32

def rms_norm(x, g):
    xf = x.astype(F32)
    y = xf * lax.rsqrt(jnp.mean(xf * xf, axis=-1, keepdims=True) + EPS)
    return (y * g.astype(F32)).astype(x.dtype)

def modulate(h, shift, scale):
    return h * (1.0 + scale) + shift

def axial_rope_tables(n):
    rows = n // GRID_W
    row_id, col_id = jnp.meshgrid(jnp.arange(rows, dtype=F32), jnp.arange(GRID_W, dtype=F32), indexing="ij")
    pos = jnp.stack([row_id.reshape(-1), col_id.reshape(-1)], axis=-1)
    quarter = HEAD_DIM // 4
    inv_freq = ROPE_THETA ** (-jnp.arange(quarter, dtype=F32) / quarter)
    ang = pos[..., None] * inv_freq
    return jnp.cos(ang), jnp.sin(ang)

def apply_axial_rope(x, cos, sin):
    B, n, H, d = x.shape
    xf = x.astype(F32).reshape(B, n, H, 2, d // 2)
    x1, x2 = xf[..., : d // 4], xf[..., d // 4:]
    c = cos[:, None]
    s = sin[:, None]
    out = jnp.concatenate([x1 * c - x2 * s, x1 * s + x2 * c], axis=-1)
    return out.reshape(B, n, H, d).astype(x.dtype)

def attend(q, k_all, v_all):
    s = jnp.einsum("bqgrd,bkgd->bgrqk", q, k_all, preferred_element_type=F32) * (HEAD_DIM ** -0.5)
    p = jax.nn.softmax(s, axis=-1).astype(v_all.dtype)
    return jnp.einsum("bgrqk,bkgd->bqgrd", p, v_all)

def latent_attention(q, k, v, kc, vc):
    B, S = q.shape[:2]
    k_all = jnp.concatenate([k, kc], axis=1)
    v_all = jnp.concatenate([v, vc], axis=1)
    nb = S // Q_BLOCK
    qb = q.reshape(B, nb, Q_BLOCK, N_KV_HEADS, Q_PER_KV, HEAD_DIM).transpose(1, 0, 2, 3, 4, 5)
    out = lax.map(lambda qblk: attend(qblk, k_all, v_all), qb)
    return out.transpose(1, 0, 2, 3, 4, 5).reshape(B, S, ATTN_WIDTH)

def context_attention(qc, kc, vc):
    B, L = qc.shape[:2]
    q = qc.reshape(B, L, N_KV_HEADS, Q_PER_KV, HEAD_DIM)
    return attend(q, kc, vc).reshape(B, L, ATTN_WIDTH)

def implicit_filter(L, w1, b1, w2, b2, w3, freq):
    t = jnp.linspace(0.0, 1.0, L, dtype=F32)[:, None]
    bands = (FILTER_EMB - 1) // 2
    w = 2.0 * math.pi * jnp.arange(L, dtype=F32) / L
    f = jnp.linspace(1e-4, bands - 1, bands, dtype=F32)
    fw = w[:, None] * f[None, :]
    z = jnp.concatenate([t, jnp.cos(fw), -jnp.sin(fw)], axis=-1)
    fr = freq.astype(F32)
    h = jnp.sin(fr * (z @ w1.astype(F32) + b1.astype(F32)))
    h = jnp.sin(fr * (h @ w2.astype(F32) + b2.astype(F32)))
    h = h @ w3.astype(F32)
    max_decay = math.log(DECAY_TARGET) / FAST_DECAY_PCT
    min_decay = math.log(DECAY_TARGET) / SLOW_DECAY_PCT
    deltas = jnp.tile(jnp.linspace(min_decay, max_decay, HYENA_WIDTH, dtype=F32), 2)
    h = h * jnp.exp(-t * jnp.abs(deltas))
    h_fwd, h_bwd = h[:, :HYENA_WIDTH], h[:, HYENA_WIDTH:]
    kern = jnp.concatenate([h_fwd, jnp.zeros((1, HYENA_WIDTH), F32), h_bwd[1:][::-1]], axis=0)
    return kern / jnp.sum(jnp.abs(kern), axis=0, keepdims=True)

def hyena_mixer(p, kern, conv_w, conv_b, bias):
    L = p.shape[1]
    C3 = p.shape[-1]
    pad = SHORT_CONV // 2
    pc = lax.conv_general_dilated(p, conv_w[:, None, :].astype(p.dtype), window_strides=(1,),
                                  padding=((pad, pad),), dimension_numbers=("NWC", "WIO", "NWC"),
                                  feature_group_count=C3) + conv_b
    x1, x2, v = jnp.split(pc, 3, axis=-1)
    u = (v * x1).astype(F32)
    U = jnp.fft.rfft(u, n=2 * L, axis=1)
    K = jnp.fft.rfft(kern, axis=0)
    y = jnp.fft.irfft(U * K[None], n=2 * L, axis=1)[:, :L]
    y = (y + u * bias.astype(F32)) * x2.astype(F32)
    return y.astype(p.dtype)

def expert_choice_ffn(h, w_router, w_gate, w_up, w_down):
    B, N, D = h.shape
    cap = CAPACITY_FACTOR * N // N_EXPERTS
    logits = jnp.einsum("bnd,de->ben", h, w_router, preferred_element_type=F32)
    aff = jax.nn.softmax(logits, axis=1)
    gates, idx = lax.top_k(aff, cap)
    xg = jax.vmap(lambda hb, ib: hb[ib])(h, idx)
    a = jnp.einsum("becd,edf->becf", xg, w_gate)
    u = jnp.einsum("becd,edf->becf", xg, w_up)
    y = jnp.einsum("becf,efd->becd", jax.nn.silu(a) * u, w_down)
    y = y * gates[..., None].astype(y.dtype)
    return jax.vmap(lambda ib, yb: jnp.zeros((N, D), yb.dtype).at[ib.reshape(-1)].add(yb.reshape(-1, D)))(idx, y)

def setup_inputs(seed: int = 0) -> dict:
    key = jax.random.key(seed)
    ks = jax.random.split(key, 25)
    nrm = jax.random.normal
    C3 = 3 * HYENA_WIDTH
    return {
        "x": nrm(ks[0], (BATCH, SEQ, D_MODEL), F32),
        "c": nrm(ks[1], (BATCH, D_MODEL), F32),
        "ctx": nrm(ks[2], (BATCH, CTX_LEN, D_MODEL), F32),
        "c_ctx": nrm(ks[3], (D_MODEL,), F32),
        "w_mod": nrm(ks[4], (DEPTH, D_MODEL, 6 * D_MODEL), F32) * (0.5 * D_MODEL ** -0.5),
        "b_mod": nrm(ks[5], (DEPTH, 6 * D_MODEL), F32) * 0.02,
        "norm1_g": 1.0 + 0.02 * nrm(ks[6], (DEPTH, D_MODEL), F32),
        "norm2_g": 1.0 + 0.02 * nrm(ks[7], (DEPTH, D_MODEL), F32),
        "w_in": nrm(ks[8], (DEPTH, D_MODEL, IN_WIDTH), F32) * D_MODEL ** -0.5,
        "w_out": nrm(ks[9], (DEPTH, MIX_WIDTH, D_MODEL), F32) * MIX_WIDTH ** -0.5,
        "q_norm_g": 1.0 + 0.02 * nrm(ks[10], (DEPTH, HEAD_DIM), F32),
        "k_norm_g": 1.0 + 0.02 * nrm(ks[11], (DEPTH, HEAD_DIM), F32),
        "conv_w": nrm(ks[12], (DEPTH, SHORT_CONV, C3), F32) * SHORT_CONV ** -0.5,
        "conv_b": nrm(ks[13], (DEPTH, C3), F32) * 0.02,
        "filt_w1": nrm(ks[14], (DEPTH, FILTER_EMB, FILTER_ORDER), F32) * FILTER_EMB ** -0.5,
        "filt_b1": nrm(ks[15], (DEPTH, FILTER_ORDER), F32) * 0.1,
        "filt_w2": nrm(ks[16], (DEPTH, FILTER_ORDER, FILTER_ORDER), F32) * FILTER_ORDER ** -0.5,
        "filt_b2": nrm(ks[17], (DEPTH, FILTER_ORDER), F32) * 0.1,
        "filt_w3": nrm(ks[18], (DEPTH, FILTER_ORDER, 2 * HYENA_WIDTH), F32) * FILTER_ORDER ** -0.5,
        "filt_freq": 1.0 + 0.1 * nrm(ks[19], (DEPTH, FILTER_ORDER), F32),
        "hyena_bias": nrm(ks[20], (DEPTH, HYENA_WIDTH), F32),
        "w_router": nrm(ks[21], (DEPTH, D_MODEL, N_EXPERTS), F32) * D_MODEL ** -0.5,
        "w_gate": nrm(ks[22], (DEPTH, N_EXPERTS, D_MODEL, D_EXPERT), F32) * D_MODEL ** -0.5,
        "w_up": nrm(ks[23], (DEPTH, N_EXPERTS, D_MODEL, D_EXPERT), F32) * D_MODEL ** -0.5,
        "w_down": nrm(ks[24], (DEPTH, N_EXPERTS, D_EXPERT, D_MODEL), F32) * D_EXPERT ** -0.5,
    }

def reference(x, c, ctx, c_ctx, w_mod, b_mod, norm1_g, norm2_g, w_in, w_out, q_norm_g, k_norm_g,
              conv_w, conv_b, filt_w1, filt_b1, filt_w2, filt_b2, filt_w3, filt_freq, hyena_bias,
              w_router, w_gate, w_up, w_down):
    B, S, _ = x.shape
    Lc = ctx.shape[1]
    cos, sin = axial_rope_tables(S)
    silu_c = jax.nn.silu(c)
    silu_cc = jax.nn.silu(c_ctx)
    splits = [ATTN_WIDTH, ATTN_WIDTH + KV_WIDTH, ATTN_WIDTH + 2 * KV_WIDTH]
    for l in range(DEPTH):
        last = l == DEPTH - 1
        mod = silu_c @ w_mod[l] + b_mod[l]
        mod_c = silu_cc @ w_mod[l] + b_mod[l]
        sh1, sc1, g1, sh2, sc2, g2 = jnp.split(mod[:, None, :], 6, axis=-1)
        csh1, csc1, cg1, csh2, csc2, cg2 = jnp.split(mod_c, 6)
        w_q, w_k, w_v, w_h = jnp.split(w_in[l], splits, axis=1)
        hx = modulate(rms_norm(x, norm1_g[l]), sh1, sc1)
        hc = modulate(rms_norm(ctx, norm1_g[l]), csh1, csc1)
        kc = rms_norm((hc @ w_k).reshape(B, Lc, N_KV_HEADS, HEAD_DIM), k_norm_g[l])
        vc = (hc @ w_v).reshape(B, Lc, N_KV_HEADS, HEAD_DIM)
        q = apply_axial_rope(rms_norm((hx @ w_q).reshape(B, S, N_Q_HEADS, HEAD_DIM), q_norm_g[l]), cos, sin)
        k = apply_axial_rope(rms_norm((hx @ w_k).reshape(B, S, N_KV_HEADS, HEAD_DIM), k_norm_g[l]), cos, sin)
        v = (hx @ w_v).reshape(B, S, N_KV_HEADS, HEAD_DIM)
        attn_x = latent_attention(q, k, v, kc, vc)
        kern_x = implicit_filter(S, filt_w1[l], filt_b1[l], filt_w2[l], filt_b2[l], filt_w3[l], filt_freq[l])
        hy_x = hyena_mixer(hx @ w_h, kern_x, conv_w[l], conv_b[l], hyena_bias[l])
        mix_x = jnp.concatenate([attn_x, hy_x], axis=-1) @ w_out[l]
        if not last:
            qc = rms_norm((hc @ w_q).reshape(B, Lc, N_Q_HEADS, HEAD_DIM), q_norm_g[l])
            attn_c = context_attention(qc, kc, vc)
            kern_c = implicit_filter(Lc, filt_w1[l], filt_b1[l], filt_w2[l], filt_b2[l], filt_w3[l], filt_freq[l])
            hy_c = hyena_mixer(hc @ w_h, kern_c, conv_w[l], conv_b[l], hyena_bias[l])
            ctx = ctx + cg1 * (jnp.concatenate([attn_c, hy_c], axis=-1) @ w_out[l])
            hc2 = modulate(rms_norm(ctx, norm2_g[l]), csh2, csc2)
            ctx = ctx + cg2 * expert_choice_ffn(hc2, w_router[l], w_gate[l], w_up[l], w_down[l])
        x = x + g1 * mix_x
        hx2 = modulate(rms_norm(x, norm2_g[l]), sh2, sc2)
        x = x + g2 * expert_choice_ffn(hx2, w_router[l], w_gate[l], w_up[l], w_down[l])
    return x


_drawn_inputs = setup_inputs


def setup_inputs(seed=0):
    import zlib

    import numpy as np

    out = dict(_drawn_inputs(seed))
    spreads = {}
    factors = {'ctx': 8.0,
     'c_ctx': 4.073,
     'norm1_g': 6.366,
     'norm2_g': 32.948,
     'q_norm_g': 64.0,
     'k_norm_g': 64.0,
     'conv_b': 6.039,
     'filt_w1': 3.495,
     'filt_b1': 8.0,
     'filt_w2': 3.201,
     'filt_b2': 8.0,
     'filt_w3': 3.404,
     'filt_freq': 8.0}
    for name, (base, spread) in spreads.items():
        noise = np.random.default_rng([zlib.crc32(name.encode()), seed]).standard_normal(out[name].shape)
        drawn = base * np.exp(spread * noise) if base else spread * noise
        out[name] = __import__('jax').numpy.asarray(drawn.astype(out[name].dtype))
    for name, factor in factors.items():
        out[name] = (out[name] * factor).astype(out[name].dtype)
    return out
```

```python
import math
from contextlib import ExitStack

import concourse.bass as bass
from concourse import mybir

P = 128
DM = 1024
SEQ = 1024
CTX = 256
DK = DM // P
TT = SEQ // P
CT = CTX // P
KT = TT + CT
HD = 64
NQ = 8
NKV = 2
NH = NQ + NKV
QW = NQ * HD
QKW = NH * HD
QKVW = QKW + NKV * HD
HYW = 512
HC = HYW // P
GRID_W = 64
EMB = 33
ORD = 64
NE = 16
CAP = 2 * SEQ // NE
FF = 2752
EPS = 1e-6
NFFT = 2 * SEQ
N1 = NFFT // 8
NCLS = 8
Q8 = math.sqrt(0.5)


def constants():
    import numpy as np
    f32 = np.float32
    n1 = np.arange(N1)
    th = 2 * np.pi / NFFT

    def ang(k2, k1):
        return th * (np.outer(n1, k2 + 8 * k1) % NFFT)
    fwd, inv = [], []
    j = np.arange(P)
    a0, a4 = ang(0, j), ang(4, j)
    nyq = np.zeros((N1, P))
    nyq[:, 0] = np.where(n1 % 2, -1.0, 1.0)
    for m in (np.cos(a0), np.sin(a0), nyq, np.cos(a4), np.sin(a4)):
        fwd.append(m)
    for k2 in (1, 2, 3):
        a = ang(k2, np.arange(N1))
        fwd += [np.cos(a), np.sin(a), -np.sin(a)]
    fwd = np.concatenate(fwd, 1).reshape(2, P, -1).transpose(1, 0, 2)
    w0 = np.full((P, 1), 2.0 / NFFT)
    w0[0] = 1.0 / NFFT
    c0, s0 = np.cos(a0).T * w0, np.sin(a0).T * w0
    s0[0] = nyq[:, 0] / NFFT
    inv += [c0, s0, np.cos(a4).T * 2 / NFFT, np.sin(a4).T * 2 / NFFT]
    for k2 in (1, 2, 3):
        a = ang(k2, np.arange(N1)).T * 1.0
        c, s = np.cos(a) * 2 / NFFT, np.sin(a) * 2 / NFFT
        for t in (0, 1):
            r = slice(t * P, t * P + P)
            inv += [np.concatenate([c[r], s[r]], 1), np.concatenate([s[r], -c[r]], 1)]
    inv = np.concatenate(inv, 1)
    t = np.linspace(0.0, 1.0, SEQ, dtype=f32)[:, None]
    bands = (EMB - 1) // 2
    w = f32(2.0 * math.pi) * np.arange(SEQ, dtype=f32) / f32(SEQ)
    f = np.linspace(1e-4, bands - 1, bands, dtype=f32)
    fw = w[:, None] * f[None, :]
    z = np.concatenate([t, np.cos(fw), -np.sin(fw)], -1).T
    dmax, dmin = math.log(1e-2) / 0.3, math.log(1e-2) / 1.5
    deltas = np.linspace(dmin, dmax, HYW, dtype=f32)
    decay = np.exp(-t * np.abs(deltas))
    quarter = HD // 4
    invf = (f32(10000.0) ** (-np.arange(quarter, dtype=f32) / f32(quarter))).astype(f32)
    tok = np.arange(SEQ)
    pos = np.stack([tok // GRID_W, tok % GRID_W], -1).astype(f32)
    an = pos[..., None] * invf
    rope = np.stack([np.cos(an), np.sin(an)], 1)
    return {
        "fwd": np.ascontiguousarray(fwd, f32), "inv": np.ascontiguousarray(inv, f32),
        "feat": np.ascontiguousarray(z, f32), "decay": np.ascontiguousarray(decay, f32),
        "rope": np.ascontiguousarray(rope.reshape(SEQ, 64), f32), "ident": np.eye(P, dtype=f32),
    }


def build(nc, t, out):
    fp32, fp32r = mybir.dt.float32, mybir.dt.float32r
    i32, u32 = mybir.dt.int32, mybir.dt.uint32
    ALU, ACT, AX = mybir.AluOpType, mybir.ActivationFunctionType, mybir.AxisListType
    ctx = ExitStack()

    def sem(name):
        return ctx.enter_context(nc.semaphore(name))

    def at(name, shape, kb, dt=fp32):
        return nc.alloc_sbuf_tensor_at(name, shape, dt, offset=int(kb * 1024) - 896)

    psum = ctx.enter_context(nc.psum_tensor("psum", [P, 8 * 512], fp32))
    bank = [psum[:, i * 512:(i + 1) * 512] for i in range(8)]

    kscr = nc.dram_tensor("kscr", [2, NCLS, P, HYW], fp32, kind="Internal").ap()

    ident = at("ident", [P, P], 17)
    cols = at("cols", [P, 132], 17.5)
    C_C, C_CC, C_G1, C_G2, C_BM, C_CW, C_CB = 0, 8, 16, 24, 32, 80, 116
    silu_c = at("silu_c", [P, DK, 2], 18.125)
    mod_t = at("mod_t", [P, 6 * DK, 2], 18.25)
    scale1 = at("scale1", [P, DK, 2], 18.75)
    scale2 = at("scale2", [P, DK], 18.875)
    rstd = at("rstd", [P, KT], 19)
    stat = at("stat", [P, 3, KT], 19.0625)
    ones = at("ones", [P, P], 19.25)
    silu_b = at("silu_b", [P, DK, P], 28)
    gate_b = at("gate_b", [P, 2, DM], 33)
    decay = at("decay", [P, TT, HYW], 41)
    hdif = at("hdif", [P, TT, HYW], 41)
    hfwd = at("hfwd", [P, TT, HYW], 57)
    hbwd = at("hbwd", [P, TT, HYW], 73)
    vsum = at("vsum", [P, 10, 2 * HYW], 89)
    vdif = at("vdif", [P, 10, 2 * HYW], 129)
    habs = at("habs", [P, 2, TT * HYW], 129)
    rows1 = at("rows1", [80, P], 89)
    rows2 = at("rows2", [52, P], 89.5)
    feat = at("feat", [EMB, SEQ], 90)
    fw1 = at("fw1", [EMB, ORD], 94)
    fw2 = at("fw2", [ORD, ORD], 94.25)
    fcol = at("fcol", [ORD, 3], 94.5)
    fw3 = at("fw3", [ORD, 2 * HYW], 95)
    farg = at("farg", [ORD, 2, 512], 99)
    fk = at("fk", [ORD, 2, 512], 103)
    fsin = at("fsin", [ORD, 2, 2, 512], 107)
    fwd = at("fwd", [P, 2, 2944], 169)
    kout = at("kout", [P, 4, HYW], 192)
    xstat = at("xstat", [P, 2, DM], 192)
    invn = at("invn", [P, HYW], 22)
    bias_b = at("bias_b", [P, HYW], 24)
    mod_row = at("mod_row", [2, 2, 256], 26)
    wmod = at("wmod", [P, 3, DK, 256], 200)

    names = """ident_in rows_in filt_in decay_in fwd_in bias_in brow_in cols_ps cols_ok silu_ok silub_ok
        l1_ps l2_ps sin_in sin_ok l3_ps h_ok habs_ok norm_ps invn_ok v_ok kps kmul kadd
        mod_ps mrow_ok mtr_ps modt_ok xs_used ssq_ok sqrt_ok var_ok ones_ok mod_done""".split()
    S = {n: sem(n) for n in names}
    wm_in = [sem(f"wm_in{i}") for i in range(3)]
    xs_in = [sem(f"xs_in{i}") for i in range(2)]
    kst = [sem(f"kst{i}") for i in range(4)]
    MU = 6 * DM // 256
    rowu = [j for j in range(MU) if j * 256 // DM not in (2, 5)]
    gatu = [j for j in range(MU) if j * 256 // DM in (2, 5)]

    C0, S0, NY, C4, S4 = 0, 128, 256, 384, 512
    V0, V4, R1, I1, R2, I2, R3, I3, VA, VB = range(10)

    def terms(side):
        out = []
        out.append([(C0, V0, 0)] if side == 0 else [(S0, V0, 0), (NY, V0, 1)])
        out.append([(C4, V4, 0)] if side == 0 else [(S4, V4, 0)])
        for k2 in (1, 2, 3):
            base = 640 + (k2 - 1) * 768
            r, i = 2 * k2, 2 * k2 + 1
            for h in (0, 128):
                out.append([(base + h, r, 0), (base + 512 + h, i, 0)] if side == 0
                           else [(base + h, i, 0), (base + 256 + h, r, 0)])
        return out

    def transform(pe, psum, side, tile, v, vnyq, fm):
        mm = [(c, w, vnyq if ny else v, j) for c, w, ny in terms(side)[tile] for j in (0, 1)]
        for n, (c, w, src, j) in enumerate(mm):
            last = pe.matmul(psum[:, :], fm[:, j, c:c + P], src[:, w, j * HYW:(j + 1) * HYW],
                             start=(n == 0), stop=(n == len(mm) - 1))
        return last

    def mod_unit(pe, n, j):
        pe.wait_ge(wm_in[n % 3], 16 * (n // 3 + 1))
        gate = j in gatu
        ps = bank[4 + n % 2]
        if n >= 2:
            pe.wait_ge(S["mrow_ok"], n - 1)
        for k in range(DK):
            lhs = silu_b[:, k, :] if gate else silu_c[:, k, :]
            last = pe.matmul(ps[0:P if gate else 2, 0:256], lhs, wmod[:, n % 3, k, :],
                             start=(k == 0), stop=(k == DK - 1) and not gate)
        if gate:
            g, o = gatu.index(j) // 4, (gatu.index(j) % 4) * 256
            pe.matmul(ps[:, 0:256], ones[0:1, :], gate_b[0:1, g, o:o + 256],
                      start=False, stop=True).then_inc(S["mod_ps"], 1)
        else:
            last.then_inc(S["mod_ps"], 1)
        return gate

    qk_all = at("qk_all", [P, KT, NH, HD], 41)
    v_all = at("v_all", [P, KT, NKV * HD], 66)
    wqkv_hi = at("wqkv_hi", [P, DK, QKVW], 71, fp32r)
    wqkv_lo = at("wqkv_lo", [P, DK, QKVW], 95, fp32r)
    xt = at("xt", [P, 2, DM], 119)
    rtmp = at("rtmp", [P, 2, NH * HD // 2], 127)
    head_g = at("head_g", [P, 2, HD], 129.5)
    hT_hi = at("hT_hi", [P, DK, SEQ], 130, fp32r)
    hT_lo = at("hT_lo", [P, DK, SEQ], 162, fp32r)
    xn = at("xn", [P, DM], 194)
    wqkv = at("wqkv", [P, DK, QKVW], 200)
    hs_hi = at("hs_hi", [P, 2, DK, P], 200, fp32r)
    hs_lo = at("hs_lo", [P, 2, DK, P], 208, fp32r)
    hfull = at("hfull", [P, DK, P], 216)
    qsq = at("qsq", [P, NH, HD], 220)
    rope = at("rope", [P, TT, 2, 2, HD // 4], 20)
    qn = at("qn", [P, NH, HD], 26)
    qst = at("qst", [P, 4, NH], 222.5)
    names1 = """wqkv_in wqkvhi_ok wqkvlo_ok small1_in xt_used xn_ok xT_ps full_ok hs_ok hT_in q_ps kv_ps sq_ok
        qvar_ok qsd_ok qn_ok qk_ok""".split()
    S.update({n: sem(n) for n in names1})
    xt_in = [sem(f"xt_in{i}") for i in range(2)]

    def need(eng, name, value):
        if not (isinstance(value, int) and value <= 0):
            eng.wait_ge(S[name], value)

    def over_tiles(eng, first, second):
        first(0, 0, 0)
        first(1, 0, 1)
        second(0, 0, 0)
        with eng.Fori(1, TT // 2) as i:
            first(i * 2, i, 0)
            second(i * 2 - 1, i - 1, 1)
            first(i * 2 + 1, i, 1)
            second(i * 2, i, 0)
        for t in range(TT, KT):
            first(t, t // 2, t % 2)
            second(t - 1, (t - 1) // 2, (t - 1) % 2)
        second(KT - 1, (KT - 1) // 2, (KT - 1) % 2)

    def is_ctx(t):
        return isinstance(t, int) and t >= TT

    def split3(pe, ps, hi, lo, w_hi, w_lo, first, last):
        pe.matmul(ps, hi, w_hi, start=first, stop=False)
        pe.matmul(ps, hi, w_lo, start=False, stop=False)
        return pe.matmul(ps, lo, w_hi, start=False, stop=last)

    x2_all = at("x2_all", [P, HC, SEQ], 71)
    uT = at("uT", [P, TT, HYW], 87)
    wh = at("wh", [P, 3, DK, P], 103)
    wh_hi = at("wh_hi", [P, 3, DK, P], 115, fp32r)
    wh_lo = at("wh_lo", [P, 3, DK, P], 194, fp32r)
    pad = at("pad", [P, 3, SEQ + 2], 206)
    gated = at("gated", [P, SEQ], 218.5)
    vconv = at("vconv", [P, SEQ], 28)
    vu = at("vu", [P, 10, 2 * HYW], 103)
    fwd3 = at("fwd3", [P, 2, 2944], 143)
    yspec = at("yspec", [P, NCLS, 2, HYW], 166)
    kin = at("kin", [P, 2, 2, HYW], 198)
    prod = at("prod", [P, 2, 4, HYW], 206)
    inv = at("inv", [P, 7168], 103)
    zs = at("zs", [P, 2, 4, 512], 131)
    ztmp = at("ztmp", [P, 8, N1], 147)
    ysum = at("ysum", [P, 4, N1], 155)
    mix_hy = at("mix_hy", [P, HC, SEQ], 208)
    names2 = """proj_ps evac_ok whhi_ok wh_ok conv_ok u_ok uT_ps uT_ok x2_ok vu_ok us_ps prod_ok y_ok
        inv_in z_ps z_ok mixhy_ok fwd3_in""".split()
    S.update({n: sem(n) for n in names2})
    wh_in = [sem(f"wh_in{i}") for i in range(3)]
    kin_in = [sem(f"kin_in{i}") for i in range(2)]
    GROUP = (2, 0, 1)

    def over_channels(eng, split, work):
        split(0)
        work(0, lambda: split(1))
        with eng.Fori(1, HC - 1) as c:
            work(c, lambda: split(c + 1))
        work(HC - 1, lambda: None)

    mix_at = at("mix_at", [P, NQ // 2, SEQ], 71)
    kT_hi = at("kT_hi", [P, NKV, KT * P], 87, fp32r)
    kT_lo = at("kT_lo", [P, NKV, KT * P], 97, fp32r)
    ks_hi = at("ks_hi", [P, KT, NKV, 2, HD], 107, fp32r)
    ks_lo = at("ks_lo", [P, KT, NKV, 2, HD], 117, fp32r)
    qs = at("qs", [P, 2, TT, 2, HD], 127, fp32r)
    qT = at("qT", [P, 2, SEQ], 135, fp32r)
    prob = at("prob", [P, 4, KT * P], 143)
    probT = at("probT", [P, 2, KT, 512], 163)
    nmax = at("nmax", [P, 4], 203)
    psums = at("psums", [P, 4], 203.125)
    prcp = at("prcp", [P, 4], 203.25)
    names3 = """kshi_ok kslo_ok kT_ps kT_ok qshi_ok qslo_ok s_ps mx_ok p_ok rs_ok pn_ok t_ps te_ok
        pv_ps pve_ok at_free""".split()
    S.update({n: sem(n) for n in names3})
    STEPS = 16
    NPAIR = NQ // 2
    LAG = 4
    KROUND = [(w, kv, a) for w in (0, 1) for kv in range(NKV) for a in (0, 4, 8)]
    TROUND = ((0, 4), (4, 8), (8, KT))
    V_SLOT = (LAG - 1, LAG + 7)
    V_BANK = 3 * (LAG % 2)

    QROUND = {3: (0, 1), 5: (1, 1), 12: (0, 0), 14: (1, 0)}

    def schedule(kind):
        rounds, k = [], -2 if kind == "tail" else 0
        for s in range(LAG if kind == "tail" else STEPS):
            now = []
            for j in range(3):
                if not (kind == "first" and s < LAG):
                    now.append((k, "p", j))
                k += 1
            if kind != "tail" and s in QROUND and not (kind == "last" and s > 8):
                now.append((k, "q") + QROUND[s])
                k += 1
            rounds.append(now)
        return rounds

    ROUNDS = {kind: schedule(kind) for kind in ("first", "mid", "last", "tail")}
    RB = ROUNDS["mid"][-1][-1][0] + 1
    BEFORE = {"mid": "mid", "last": "mid", "tail": "last"}

    def thirds_done(kind, s):
        if s < 0:
            return thirds_done(BEFORE[kind], s + STEPS) - RB
        return [r[0] for r in ROUNDS[kind][s] if r[1] == "p"][-1]

    def over_pairs(eng, body):
        body(0, "first")
        with eng.Fori(1, NPAIR - 1) as r:
            body(r, "mid")
        body(NPAIR - 1, "last")
        body(NPAIR, "tail")

    wo_hi = at("wo_hi", [P, DK, DM], 87, fp32r)
    wo_lo = at("wo_lo", [P, DK, DM], 119, fp32r)
    wo = at("wo", [P, 4, DM], 151)
    ms_hi = at("ms_hi", [P, 2, DK, P], 167, fp32r)
    ms_lo = at("ms_lo", [P, 2, DK, P], 175, fp32r)
    xr = at("xr", [P, 2, DM], 41)
    x1 = at("x1", [P, 2, DM], 49)
    xn2 = at("xn2", [P, 2, DM], 57)
    junk = at("junk", [P, DM], 183)
    gmix = at("gmix", [P, DM], 187)
    hs2 = at("hs2", [P, 2, DK, P], 191)
    aff = at("aff", [NE, 2, SEQ], 200)
    top_v = at("top_v", [NE, CAP], 26)
    top_i = at("top_i", [NE, CAP], 26.5, u32)
    top_f = at("top_f", [NE, CAP], 27)
    w_r = at("w_r", [P, DK, NE], 28)
    aff_t = at("aff_t", [P, TT, NE], 28.5)
    slot_i = at("slot_i", [P, NE + 1], 29, u32)
    slot_g = at("slot_g", [P, NE], 29.125)
    idx = at("idx", [P, 2], 29.25, u32)
    st2 = at("st2", [P, 8, 2], 29.375)
    idx_out = at("idx_out", [P, 1], 29.5, u32)
    zero_i = at("zero_i", [P, 1], 29.5625, u32)
    xscr = nc.dram_tensor("xscr", [SEQ, DM], fp32, kind="Internal").ap()
    FB = 384
    NB = FF // FB
    FL = FF - (NB - 1) * FB
    wraw = at("wraw", [P, 4, DK, FL], 41)
    we_hi = at("we_hi", [P, 2, DK, FL], 97, fp32r)
    we_lo = at("we_lo", [P, 2, DK, FL], 125, fp32r)
    wdn = at("wdn", [P, 2, 4, DM], 153)
    xg = at("xg", [P, DM], 185)
    xf = at("xf", [P, DK, P], 189)
    xe_hi = at("xe_hi", [P, 2, DK, P], 193, fp32r)
    xe_lo = at("xe_lo", [P, 2, DK, P], 201, fp32r)
    sil = at("sil", [P, FL], 209)
    hid = at("hid", [P, 2, FL], 210.75)
    hidT = at("hidT", [P, 2, 4, P], 214.25)
    yb = at("yb", [P, DM], 218.25)
    names4 = """wohi_ok wo_ok mshi_ok ms_ok o_ps x1_ok ssq2_ok var2_ok sd2_ok xn2_ok x2T_ps hx2_ok r_ps rmx_ok
        rexp_ok aff_ok affT_ps affT_ok small2_in top_ok tops_ps slots_ok
        hi_ok lo_ok gu_ps sil_ok hid_ok hidT_ps hidT_ok d_ps ye_ok scat gat xx_ps xf_ok xe_ok""".split()
    S.update({n: sem(n) for n in names4})
    wo_in = [sem(f"wo_in{i}") for i in range(4)]
    xr_in = [sem(f"xr_in{i}") for i in range(2)]
    xst = [sem(f"xst{i}") for i in range(2)]
    wraw_in = [sem(f"wraw_in{i}") for i in range(4)]
    wdn_in = [sem(f"wdn_in{i}") for i in range(2)]

    def over_out(eng, first, second):
        first(0, 0, 0)
        first(1, 0, 1)
        second(0, 0, 0)

        def two(i):
            first(i * 2, i, 0)
            second(i * 2 - 1, i - 1, 1)
            first(i * 2 + 1, i, 1)
            second(i * 2, i, 0)

        with eng.Fori(1, TT // 2 - 1) as i:
            two(i)
        two(TT // 2 - 1)
        second(TT - 1, TT // 2 - 1, 1)

    def over_experts(eng, body):
        body(0)
        with eng.Fori(1, NE // 2) as i:
            body(i)

    width = lambda b: FL if b == NB - 1 else FB
    chunks = lambda b: [(j, min(P, width(b) - j * P)) for j in range((width(b) + P - 1) // P)]
    BLOCKS = [(ee, b) for ee in (0, 1) for b in range(NB)]

    DN_AT, DN_TOTAL = [], [0, 0]
    for n, (_, b) in enumerate(BLOCKS):
        DN_TOTAL[n % 2] += 2 if b == NB - 1 else 1
        DN_AT.append(DN_TOTAL[n % 2])

    block = ctx.enter_context(nc.Block())

    @block.sync
    def _(sp):
        sp.dma_start(ident[:, :], t["ident"]).then_inc(S["ident_in"], 16)
        r128 = lambda a: a.rearrange("(r p) -> r p", p=P)
        for dst, src in ((rows1[0:8], r128(t["c"][0])), (rows1[8:16], r128(t["c_ctx"])),
                         (rows1[16:24], r128(t["norm1_g"][0])), (rows1[24:32], r128(t["norm2_g"][0])),
                         (rows1[32:80], r128(t["b_mod"][0])),
                         (rows2[0:36], t["conv_w"][0].rearrange("t (r p) -> (t r) p", p=P)),
                         (rows2[36:48], r128(t["conv_b"][0])), (rows2[48:52], r128(t["hyena_bias"][0]))):
            sp.dma_start(dst, src).then_inc(S["rows_in"], 16)
        one = lambda a: a.rearrange("(p o) -> p o", o=1)
        with nc.allow_non_contiguous_dma(reason="three columns of 64"):
            for dst, src in ((feat[:, :], t["feat"]), (fw1[:, :], t["filt_w1"][0]), (fw2[:, :], t["filt_w2"][0]),
                             (fcol[:, 0:1], one(t["filt_b1"][0])), (fcol[:, 1:2], one(t["filt_b2"][0])),
                             (fcol[:, 2:3], one(t["filt_freq"][0])), (fw3[:, :], t["filt_w3"][0])):
                sp.dma_start(dst, src).then_inc(S["filt_in"], 16)
        sp.dma_start(decay[:, :, :], t["decay"].rearrange("(t p) c -> p t c", p=P)).then_inc(S["decay_in"], 16)
        sp.dma_start(bias_b[:, :], t["hyena_bias"][0:1, :].to_broadcast([P, HYW])).then_inc(S["bias_in"], 16)
        for g, o in ((0, 2 * DM), (1, 5 * DM)):
            sp.dma_start(gate_b[0:1, g, :], t["b_mod"][0:1, o:o + DM]).then_inc(S["brow_in"], 16)

        def load_wmod(n):
            j = (rowu[:8] + gatu + rowu[8:])[n]
            if n >= 3:
                sp.wait_ge(S["mod_ps"], n - 2)
            sp.dma_start(wmod[:, n % 3, :, :],
                         t["w_mod"][0, :, j * 256:(j + 1) * 256].rearrange("(k p) c -> p k c", p=P)
                         ).then_inc(wm_in[n % 3], 16)

        for n in range(3):
            load_wmod(n)
        sp.dma_start(fwd[:, :, :], t["fwd"]).then_inc(S["fwd_in"], 16)
        for n in range(3, MU):
            load_wmod(n)

        sp.wait_ge(S["mod_ps"], MU)
        for k in range(0, DK, 2):
            sp.dma_start(wqkv[:, k:k + 2, :], t["w_in"][0, k * P:(k + 2) * P, 0:QKVW].rearrange(
                "(k p) c -> p k c", p=P)).then_inc(S["wqkv_in"], 16)
        sp.dma_start(rope[:, :, :, :, :].rearrange("p t a b c -> p t (a b c)"),
                     t["rope"].rearrange("(t p) c -> p t c", p=P)).then_inc(S["small1_in"], 16)
        sp.dma_start(head_g[:, 0, :], t["q_norm_g"][0:1, :].to_broadcast([P, HD])).then_inc(S["small1_in"], 16)
        sp.dma_start(head_g[:, 1, :], t["k_norm_g"][0:1, :].to_broadcast([P, HD])).then_inc(S["small1_in"], 16)

        def load_x(i, h, par):
            sp.wait_ge(S["xt_used"], i + 1)
            src = t["ctx"][0, bass.ts(i - TT, P), :] if is_ctx(i) else t["x"][0, bass.ts(i, P), :]
            sp.dma_start(xt[:, par, :], src).then_inc(xt_in[par], 16)

        def copy_h(i, h, par):
            if is_ctx(i):
                return
            sp.wait_ge(S["hs_ok"], i + 1)
            for dst, src in ((hT_hi, hs_hi), (hT_lo, hs_lo)):
                sp.dma_start(dst[:, :, bass.ts(i, P)].bitcast(fp32), src[:, par, :, :].bitcast(fp32)).then_inc(S["hT_in"], 16)

        over_tiles(sp, load_x, copy_h)

        sp.wait_ge(S["kv_ps"], KT + 2)

        def load_wh(c):
            for g in range(3):
                sp.wait_ge(S["wh_ok"], c * 3 + g + 1)
                sp.dma_start(wh[:, g, :, :], t["w_in"][0, :, bass.ds(c * P + (QKVW + GROUP[g] * HYW), P)].rearrange(
                    "(k p) c -> p k c", p=P)).then_inc(wh_in[g], 16)

        over_channels(sp, load_wh, lambda c, ahead: ahead())
        sp.wait_ge(S["uT_ok"], HC + 1)
        sp.wait_ge(S["proj_ps"], 6 * HC + 6)
        sp.dma_start(fwd3[:, :, :], t["fwd"]).then_inc(S["fwd3_in"], 16)
        sp.wait_ge(S["x2_ok"], HC)
        for i in range(NCLS):
            if i >= 2:
                sp.wait_ge(S["prod_ok"], i - 1)
            for side in (0, 1):
                sp.dma_start(kin[:, i % 2, side, :], kscr[side, i, :, :]).then_inc(kin_in[i % 2], 16)
        sp.wait_ge(S["us_ps"], 2 * NCLS)
        sp.dma_start(inv[:, :], t["inv"]).then_inc(S["inv_in"], 16)


        sp.wait_ge(S["pve_ok"], 2 * NPAIR)
        def load_wo(k):
            if k >= 4:
                sp.wait_ge(S["wo_ok"], k - 3)
            if k < NPAIR:
                for w in (0, 1):
                    r0 = (k + 4 * w) * HD
                    sp.dma_start(wo[w * HD:(w + 1) * HD, k % 4, :], t["w_out"][0, r0:r0 + HD, :]
                                 ).then_inc(wo_in[k % 4], 16)
            else:
                sp.dma_start(wo[:, k % 4, :], t["w_out"][0, k * P:(k + 1) * P, :]).then_inc(wo_in[k % 4], 16)

        for k in range(4):
            load_wo(k)
        sp.dma_start(w_r[:, :, :], t["w_router"][0].rearrange("(k p) e -> p k e", p=P)).then_inc(S["small2_in"], 16)
        for k in range(4, DK):
            load_wo(k)

        def load_xr(i, h, par):
            need(sp, "x1_ok", i - 1)
            sp.dma_start(xr[:, par, :], t["x"][0, bass.ts(i, P), :]).then_inc(xr_in[par], 16)

        def store(i, h, par):
            sp.wait_ge(S["xn2_ok"], i + 1)
            sp.dma_start(out[0, bass.ts(i, P), :], x1[:, par, :]).then_inc(xst[par], 16)
            sp.dma_start(xscr[bass.ts(i, P), :], xn2[:, par, :]).then_inc(xst[par], 16)

        over_out(sp, load_xr, store)
        for i in (0, 1):
            sp.wait_ge(xst[i], 16 * TT + 32)
        sp.wait_ge(S["o_ps"], TT)
        sp.wait_ge(S["hx2_ok"], TT)

        def load_down(i, n):
            ee, b = (-1, NB - 1) if n < 0 else BLOCKS[n]
            w, c0 = width(b), b * FB
            need(sp, "d_ps", i * 14 + (n - 1))
            full = w // P
            wd = t["w_down"][0, bass.ds(i * 2 + ee, 1), :, :].squeeze(0)
            sp.dma_start(wdn[:, n % 2, 0:full, :], wd[c0:c0 + full * P, :].rearrange("(j p) c -> p j c", p=P)
                         ).then_inc(wdn_in[n % 2], 16)
            if w % P:
                sp.dma_start(wdn[0:w % P, n % 2, full, :], wd[c0 + full * P:c0 + w, :]).then_inc(wdn_in[n % 2], 16)

        def load_experts(i):
            for n, (ee, b) in enumerate(BLOCKS):
                w, c0 = width(b), b * FB
                for m, name in ((0, "w_gate"), (1, "w_up")):
                    u = 2 * n + m
                    need(sp, "lo_ok", i * 28 + (u - 3))
                    sp.dma_start(wraw[:, u % 4, :, 0:w],
                                 t[name][0, bass.ds(i * 2 + ee, 1), :, c0:c0 + w].squeeze(0).rearrange(
                                     "(k p) c -> p k c", p=P)).then_inc(wraw_in[u % 4], 16)
                if not (isinstance(i, int) and n == 0):
                    load_down(i, n - 1)

        over_experts(sp, load_experts)
        load_down(NE // 2, -1)
        sp.wait_ge(S["scat"], 16 * NE)

    @block.gpsimd
    def _(pool):
        for i in range(KT):
            if i >= 2:
                pool.wait_ge(S["xs_used"], i - 1)
            src = t["x"][0, i * P:(i + 1) * P, :] if i < TT else t["ctx"][0, (i - TT) * P:(i - TT + 1) * P, :]
            pool.dma_start(xstat[:, i % 2, :], src).then_inc(xs_in[i % 2], 16)
        for n in range(2 * NCLS):
            if n < NCLS:
                pool.wait_ge(S["kadd"], n + 1)
            else:
                pool.wait_ge(S["kmul"], n + 1)
            pool.dma_start(kscr[n // NCLS, n % NCLS, :, :], kout[:, n % 4, :]).then_inc(kst[n % 4], 16)
        for i in range(4):
            pool.wait_ge(kst[i], 16 * NCLS // 2)

        pool.wait_ge(S["small1_in"], 48)
        pool.tensor_scalar(head_g[:, 0, :], head_g[:, 0, :], HD ** -0.5, None, ALU.mult)
        pool.drain()

        def nothing(i, h, par):
            pass

        def turn(i, h, par):
            pool.wait_ge(S["qn_ok"], i + 3)
            if is_ctx(i):
                pool.tensor_tensor(qk_all[:, bass.ds(i, 1), NQ:NH, :].squeeze(1), qn[:, NQ:NH, :],
                                   head_g[:, 1:2, :].to_broadcast([P, NKV, HD]), ALU.mult).then_inc(S["qk_ok"], 1)
                return
            for w, a, b in ((0, 0, NQ), (1, NQ, NH)):
                pool.tensor_tensor(qn[:, a:b, :], qn[:, a:b, :], head_g[:, w:w + 1, :].to_broadcast([P, b - a, HD]),
                                   ALU.mult)
            pool.drain()
            xin = qn[:, :, :].rearrange("p n (a b c) -> p n a b c", a=2, b=2)
            yout = qk_all[:, bass.ds(i, 1), :, :].squeeze(1).rearrange("p n (a b c) -> p n a b c", a=2, b=2)
            tmp = [rtmp[:, w, :].rearrange("p (n a c) -> p n a c", n=NH, a=2) for w in (0, 1)]
            tab = [rope[:, bass.ds(i, 1), w, :, :].to_broadcast([P, NH, 2, HD // 4]) for w in (0, 1)]
            x1, x2 = xin[:, :, :, 0, :], xin[:, :, :, 1, :]
            for half, (u0, u1, op) in enumerate(((0, 1, ALU.subtract), (1, 0, ALU.add))):
                pool.tensor_tensor(tmp[0], x1, tab[u0], ALU.mult)
                pool.tensor_tensor(tmp[1], x2, tab[u1], ALU.mult)
                pool.drain()
                last = pool.tensor_tensor(yout[:, :, :, half, :], tmp[0], tmp[1], op)
                if half == 0:
                    pool.drain()
            last.then_inc(S["qk_ok"], 1)

        over_tiles(pool, nothing, turn)

        for i in range(NCLS):
            pool.wait_ge(S["prod_ok"], i + 1)
            pr = prod[:, i % 2, :, :]
            pool.tensor_tensor(yspec[:, i, 0, :], pr[:, 0, :], pr[:, 1, :], ALU.subtract)
            last = pool.tensor_tensor(yspec[:, i, 1, :], pr[:, 2, :], pr[:, 3, :], ALU.add)
            if i == 0:
                pool.drain()
                for w in (0, 1):
                    last = pool.tensor_copy(yspec[0:1, i, w, :], prod[0:1, 0, w, :])
            last.then_inc(S["y_ok"], 1)

        with pool.Fori(0, NPAIR * STEPS // 4) as g:
            for m in range(4):
                pool.wait_ge(S["rs_ok"], g * 4 + m + 1)
                pool.tensor_tensor(prob[:, m, :], prob[:, m, :], prcp[:, m:m + 1].to_broadcast([P, KT * P]),
                                   ALU.mult).then_inc(S["pn_ok"], 1)

        off = lambda a: bass.IndirectOffsetOnAxis(ap=a, axis=0)
        pool.wait_ge(S["slots_ok"], 1)
        for i in (0, 1):
            pool.wait_ge(xst[i], 16 * TT + 32)

        pool.memset(zero_i[:, :], 0)
        pool.drain()

        def gather(e, slot):
            pool.tensor_copy(idx[:, slot:slot + 1], slot_i[:, bass.ds(e, 1)])
            pool.drain()
            pool.indirect_dma_start(xg[:, :], None, xscr, off(idx[:, slot:slot + 1])).then_inc(S["gat"], 16)

        gather(0, 0)

        def experts(i):
            for ee in (0, 1):
                e = i * 2 + ee
                need(pool, "xx_ps", e * 2 + 2)
                need(pool, "scat", e * 16)
                gather(e + 1, 1 - ee)
                pool.wait_ge(S["ye_ok"], e + 1)
                pool.tensor_tensor(idx_out[:, :], idx[:, ee:ee + 1], zero_i[:, :], ALU.add)
                pool.drain()
                pool.indirect_dma_start(out[0], off(idx_out[:, :]), yb[:, :], None, compute_op=ALU.add
                                        ).then_inc(S["scat"], 16)

        over_experts(pool, experts)
        pool.wait_ge(S["gat"], 16 * (NE + 1))

    @block.tensor
    def _(pe):
        pe.wait_ge(S["ident_in"], 16)
        pe.wait_ge(S["rows_in"], 8 * 16)
        pe.transpose(bank[7][:, 0:80], rows1[:, :], ident[0:80, 0:80])
        pe.transpose(bank[7][:, 80:132], rows2[:, :], ident[0:52, 0:52]).then_inc(S["cols_ps"], 1)
        pe.wait_ge(S["filt_in"], 7 * 16)
        for h in (0, 1):
            last = pe.matmul(bank[h][0:ORD, :], fw1[:, :], feat[:, h * 512:(h + 1) * 512], start=True, stop=True)
        last.then_inc(S["l1_ps"], 1)
        pe.wait_ge(S["sin_ok"], 1)
        for h in (0, 1):
            last = pe.matmul(bank[2 + h][0:ORD, :], fw2[:, :], fsin[:, 0, h, :], start=True, stop=True)
        last.then_inc(S["l2_ps"], 1)
        pe.wait_ge(S["sin_ok"], 2)
        for i in range(2 * TT):
            tt, side = i // 2, i % 2
            if i >= 4:
                pe.wait_ge(S["h_ok"], i - 3)
            pe.matmul(bank[i % 4][:, :], fsin[:, 1, tt // 4, (tt % 4) * P:(tt % 4 + 1) * P],
                      fw3[:, side * HYW:(side + 1) * HYW], start=True, stop=True).then_inc(S["l3_ps"], 1)
        order = rowu[:8] + gatu + rowu[8:]

        def unit(n):
            gate = mod_unit(pe, n, order[n])
            if not gate:
                pe.wait_ge(S["mrow_ok"], n + 1)
                m = order.index(order[n]) if n < 8 else n - 8
                if m >= 1:
                    pe.wait_ge(S["modt_ok"], m)
                for h in (0, 1):
                    last = pe.transpose(bank[7][:, 2 * h:2 * h + 2], mod_row[:, n % 2, h * P:(h + 1) * P],
                                        ident[0:2, 0:2])
                last.then_inc(S["mtr_ps"], 1)

        pe.wait_ge(S["habs_ok"], 1)
        pe.wait_ge(S["ones_ok"], 1)
        for i in range(2 * TT):
            last = pe.matmul(bank[6][:, :], ones[:, :], habs[:, i // TT, (i % TT) * HYW:(i % TT + 1) * HYW],
                             start=(i == 0), stop=(i == 2 * TT - 1))
        last.then_inc(S["norm_ps"], 1)
        pe.wait_ge(S["silu_ok"], 1)
        for n in range(8):
            unit(n)
        pe.wait_ge(S["fwd_in"], 16)
        pe.wait_ge(S["h_ok"], 2 * TT)
        for i in range(2 * NCLS):
            side, tile = i // NCLS, i % NCLS
            pe.wait_ge(S["v_ok"], side + 1)
            if i >= 4:
                pe.wait_ge(S["kmul"], i - 3)
            transform(pe, bank[i % 4], side, tile, (vsum, vdif)[side], vsum, fwd).then_inc(S["kps"], 1)
        pe.wait_ge(S["silub_ok"], 1)
        pe.wait_ge(S["brow_in"], 2 * 16)
        for n in range(8, MU):
            unit(n)


        def x_transposes(i, h, par):
            pe.wait_ge(S["xn_ok"], i + 1)
            pe.wait_ge(S["full_ok"], i + 1)
            for k in range(DK):
                last = pe.transpose(bank[k // 4][:, (k % 4) * P:(k % 4 + 1) * P], xn[:, k * P:(k + 1) * P],
                                    ident[:, :])
            last.then_inc(S["xT_ps"], 1)

        def qkv(i, h, par):
            pe.wait_ge(S["hs_ok"], i + 1)
            pe.wait_ge(S["qn_ok"], i + 1)
            parts = [(bank[4 + par], QW, QKVW, "kv_ps")]
            if not is_ctx(i):
                parts.insert(0, (bank[2 + par], 0, QW, "q_ps"))
            for ps, a, b, s in parts:
                for k in range(DK):
                    last = split3(pe, ps[:, 0:b - a], hs_hi[:, par, k, :], hs_lo[:, par, k, :],
                                  wqkv_hi[:, k, a:b], wqkv_lo[:, k, a:b], k == 0, k == DK - 1)
                last.then_inc(S[s], 1)

        pe.wait_ge(S["wqkvlo_ok"], DK)
        over_tiles(pe, x_transposes, qkv)

        def hyena_products(c, ahead):
            for g in range(3):
                pe.wait_ge(S["wh_ok"], c * 3 + g + 4)
                for h in (0, 1):
                    n = 2 * g + h
                    pe.wait_ge(S["evac_ok"], c * 6 + n + 1)
                    for k in range(DK):
                        last = split3(pe, bank[n][:, :], wh_hi[:, g, k, :], wh_lo[:, g, k, :],
                                      hT_hi[:, k, h * 512:(h + 1) * 512], hT_lo[:, k, h * 512:(h + 1) * 512],
                                      k == 0, k == DK - 1)
                    last.then_inc(S["proj_ps"], 1)
            pe.wait_ge(S["u_ok"], c + 1)
            pe.wait_ge(S["uT_ok"], c + 1)
            for tt in range(TT):
                last = pe.transpose(bank[6 + tt // 4][:, (tt % 4) * P:(tt % 4 + 1) * P],
                                    gated[:, tt * P:(tt + 1) * P], ident[:, :])
            last.then_inc(S["uT_ps"], 1)

        pe.wait_ge(S["hT_in"], 64 + 32 * TT)
        pe.wait_ge(S["full_ok"], KT + 1)
        pe.wait_ge(S["qn_ok"], KT + 2)
        over_channels(pe, lambda c: None, hyena_products)
        pe.wait_ge(S["uT_ok"], HC + 1)
        pe.wait_ge(S["evac_ok"], 6 * HC + 6)
        pe.wait_ge(S["vu_ok"], 1)
        pe.wait_ge(S["fwd3_in"], 16)
        for i in range(NCLS):
            if i >= 4:
                pe.wait_ge(S["prod_ok"], i - 3)
            for side in (0, 1):
                transform(pe, bank[2 * (i % 4) + side], side, i, vu, vu, fwd3).then_inc(S["us_ps"], 1)
        pe.wait_ge(S["prod_ok"], NCLS)
        pe.wait_ge(S["inv_in"], 16)
        for c in range(HC):
            ch = slice(c * P, (c + 1) * P)
            if c >= 2:
                pe.wait_ge(S["z_ok"], c - 1)
            zb = [bank[4 * (c % 2) + z] for z in range(4)]
            pe.wait_ge(S["y_ok"], NCLS)
            for tile in (0, 1):
                for w in (0, 1):
                    col = (2 * tile + w) * N1
                    pe.matmul(zb[0][:, tile * N1:(tile + 1) * N1], yspec[:, tile, w, ch], inv[:, col:col + N1],
                              start=(w == 0), stop=(w == 1))
            for k2 in (1, 2, 3):
                for m in range(4):
                    tile, w = 2 * k2 + m // 2, m % 2
                    col = 4 * N1 + ((k2 - 1) * 4 + m) * 512
                    last = pe.matmul(zb[k2][:, :], yspec[:, tile, w, ch], inv[:, col:col + 512],
                                     start=(m == 0), stop=(m == 3))
            last.then_inc(S["z_ps"], 1)

        pe.wait_ge(S["kshi_ok"], 1)
        pe.wait_ge(S["kslo_ok"], 1)
        pe.wait_ge(S["z_ok"], HC)
        for n, (w, kv, a) in enumerate(KROUND):
            if n >= 2:
                pe.wait_ge(S["kT_ok"], n - 1)
            for j in range(a, min(a + 4, KT)):
                last = pe.transpose(bank[6 + n % 2][:, (j - a) * P:(j - a + 1) * P],
                                    (ks_hi, ks_lo)[w][:, j, kv, :, :].rearrange("p a b -> p (a b)").bitcast(fp32),
                                    ident[:, :])
            last.then_inc(S["kT_ps"], 1)

        def q_round(r, hh, half, ps):
            pe.wait_ge(S["qslo_ok"], r * 2 + hh + 1)
            for j in range(4):
                last = pe.transpose(ps[:, j * P:(j + 1) * P],
                                    qs[:, hh, 4 * half + j, :, :].rearrange("p a b -> p (a b)").bitcast(fp32),
                                    ident[:, :])
            return last

        for hh in (0, 1):
            pe.wait_ge(S["kT_ok"], len(KROUND) + hh - 1)
            q_round(0, hh, 0, bank[6 + hh]).then_inc(S["kT_ps"], 1)
        pe.wait_ge(S["kT_ok"], len(KROUND) + 2)

        def scores(s, j, a, z):
            half, hh, qt = s // 8, s // 4 % 2, s % 4
            ps = bank[3 * (s % 2) + j][:, 0:(z - a) * P]
            q = qT[:, hh, (4 * half + qt) * P:(4 * half + qt + 1) * P]
            pe.matmul(ps, q, kT_hi[:, hh, a * P:z * P], start=True, stop=False)
            return pe.matmul(ps, q, kT_lo[:, hh, a * P:z * P], start=False, stop=True)

        def values(r, s):
            for kt in range(KT):
                for hh in (0, 1):
                    last = pe.matmul(bank[V_BANK][hh * HD:(hh + 1) * HD, :], v_all[:, kt, hh * HD:(hh + 1) * HD],
                                     probT[:, hh, kt, :], start=(kt == 0), stop=(kt == KT - 1))
            last.then_inc(S["pv_ps"], 1)

        def attend(r, kind):
            for s, rounds in enumerate(ROUNDS[kind]):
                def transposes(n):
                    if n >= len(rounds):
                        return
                    k, what = rounds[n][:2]
                    pe.wait_ge(S["te_ok"], r * RB + (k - 1))
                    if what == "p":
                        b, (a, z) = (s - LAG) % STEPS, TROUND[n]
                        if n == 0:
                            pe.wait_ge(S["pn_ok"], r * STEPS + (s - LAG + 1))
                        for kt in range(a, z):
                            last = pe.transpose(bank[6 + k % 2][:, (kt - a) * P:(kt - a + 1) * P],
                                                prob[:, b % 4, kt * P:(kt + 1) * P], ident[:, :])
                    else:
                        hh, half = rounds[n][2:]
                        last = q_round(r + (1 - half), hh, half, bank[6 + k % 2])
                    last.then_inc(S["t_ps"], 1)

                transposes(0)
                transposes(1)
                if kind != "tail":
                    pe.wait_ge(S["p_ok"], r * STEPS + s + 1)
                    if s == 0 and kind != "first":
                        pe.wait_ge(S["te_ok"], r * RB + (ROUNDS["mid"][14][-1][0] - RB + 1))
                    if s == 8:
                        pe.wait_ge(S["te_ok"], r * RB + (ROUNDS[kind][5][-1][0] + 1))
                    if s == V_SLOT[1] + 1 or (s == V_SLOT[0] + 1 and kind != "first"):
                        pe.wait_ge(S["pve_ok"], r * 2 + (s > 8))
                    scores(s, 0, *TROUND[0])
                transposes(2)
                if kind != "tail":
                    scores(s, 1, *TROUND[1])
                    scores(s, 2, *TROUND[2]).then_inc(S["s_ps"], 1)
                transposes(3)
                if s == V_SLOT[1] or (s == V_SLOT[0] and kind != "first"):
                    pe.wait_ge(S["te_ok"], r * RB + (thirds_done(kind, s) + 1))
                    if kind != "tail":
                        pe.wait_ge(S["p_ok"], r * STEPS + (s + 2))
                    values(r, s)

        over_pairs(pe, attend)

        pe.wait_ge(S["pve_ok"], 2 * NPAIR)
        pe.wait_ge(S["te_ok"], NPAIR * RB - 2 + 3 * LAG)
        pe.wait_ge(S["p_ok"], NPAIR * STEPS + 2)

        def project(i, h, par):
            pe.wait_ge(S["ms_ok"], i + 1)
            need(pe, "x1_ok", i - 1)
            for half in (0, 1):
                for k in range(DK):
                    if isinstance(i, int) and i == 0 and half == 0:
                        pe.wait_ge(S["wo_ok"], k + 1)
                    last = split3(pe, bank[2 * par + half][:, :], ms_hi[:, par, k, :], ms_lo[:, par, k, :],
                                  wo_hi[:, k, half * 512:(half + 1) * 512], wo_lo[:, k, half * 512:(half + 1) * 512],
                                  k == 0, k == DK - 1)
            last.then_inc(S["o_ps"], 1)

        def route(i, h, par):
            pe.wait_ge(S["xn2_ok"], i + 1)
            need(pe, "hx2_ok", i)
            for k in range(DK):
                last = pe.transpose(bank[4 + k // 4][:, (k % 4) * P:(k % 4 + 1) * P], xn2[:, par, k * P:(k + 1) * P],
                                    ident[:, :])
            last.then_inc(S["x2T_ps"], 1)
            pe.wait_ge(S["hx2_ok"], i + 1)
            need(pe, "rexp_ok", i)
            if isinstance(i, int) and i == 0:
                pe.wait_ge(S["small2_in"], 16)
            for k in range(DK):
                last = pe.matmul(bank[6][:, 0:NE], hs2[:, par, k, :], w_r[:, k, :], start=(k == 0), stop=(k == DK - 1))
            last.then_inc(S["r_ps"], 1)

        pe.wait_ge(S["small2_in"], 16)
        over_out(pe, project, route)
        pe.wait_ge(S["aff_ok"], TT)
        for i in range(TT):
            last = pe.transpose(bank[4 + i // 4][0:NE, (i % 4) * P:(i % 4 + 1) * P], aff_t[:, i, :], ident[:, :])
        last.then_inc(S["affT_ps"], 1)
        pe.wait_ge(S["top_ok"], 1)
        pe.transpose(bank[6][:, 0:NE], top_f[:, :], ident[0:NE, 0:NE])
        pe.transpose(bank[6][:, NE:2 * NE], top_v[:, :], ident[0:NE, 0:NE]).then_inc(S["tops_ps"], 1)
        def token_transposes(e, q, ps):
            pe.wait_ge(S["gat"], e * 16 + 16)
            for k in range(4):
                last = pe.transpose(ps[:, k * P:(k + 1) * P], xg[:, (4 * q + k) * P:(4 * q + k + 1) * P], ident[:, :])
            last.then_inc(S["xx_ps"], 1)

        def unit(i, n, ee, b, m):
            u, w = 2 * n + m, width(b)
            pe.wait_ge(S["lo_ok"], i * 28 + (u + 1))
            if m == 0:
                need(pe, "hid_ok", i * 14 + (n - 1))
                if b == 0:
                    pe.wait_ge(S["xe_ok"], i * 2 + (ee + 1))
            for k in range(DK):
                last = split3(pe, bank[2 * (n % 2) + m][:, 0:w], xe_hi[:, ee, k, :], xe_lo[:, ee, k, :],
                              we_hi[:, m, k, 0:w], we_lo[:, m, k, 0:w], k == 0, k == DK - 1)
            last.then_inc(S["gu_ps"], 1)

        def hidden_transposes(i, n, b):
            pe.wait_ge(S["hid_ok"], i * 14 + (n + 1))
            need(pe, "hidT_ok", i * 14 + (n - 1))
            if b in (3, 4):
                e = i * 2 + (1 if n >= NB else 0)
                pe.wait_ge(S["xf_ok"], e * 2 + (b))
            for j, c in chunks(b):
                last = pe.transpose(bank[4 + n % 2][0:c, j * P:(j + 1) * P], hid[:, n % 2, j * P:j * P + c], ident[:, :])
            last.then_inc(S["hidT_ps"], 1)

        def down(i, n, b):
            pe.wait_ge(S["hidT_ok"], i * 14 + (n + 1))
            if n < 0:
                pe.wait_ge(wdn_in[1], i * (16 * DN_TOTAL[1]))
            else:
                pe.wait_ge(wdn_in[n % 2], i * (16 * DN_TOTAL[n % 2]) + 16 * DN_AT[n])
            if b == 0:
                need(pe, "ye_ok", i * 2 + (1 if n >= NB else 0))
            for j, c in chunks(b):
                for half in (0, 1):
                    last = pe.matmul(bank[6 + half][:, :], hidT[0:c, n % 2, j, :],
                                     wdn[0:c, n % 2, j, half * 512:(half + 1) * 512],
                                     start=(b == 0 and j == 0), stop=(b == NB - 1 and j == len(chunks(b)) - 1))
            last.then_inc(S["d_ps"], 1)

        def experts(i):
            for n, (ee, b) in enumerate(BLOCKS):
                before = not (isinstance(i, int) and i == 0 and n == 0)
                pb = BLOCKS[n - 1][1]
                unit(i, n, ee, b, 0)
                if before:
                    hidden_transposes(i, n - 1, pb)
                unit(i, n, ee, b, 1)
                if before:
                    down(i, n - 1, pb)
                if b in (2, 3):
                    token_transposes(i * 2 + (ee + 1), b - 2, bank[4 + (n - 1) % 2])

        pe.wait_ge(S["affT_ok"], 1)
        for q in (0, 1):
            token_transposes(0, q, bank[4 + q])
        pe.wait_ge(S["xf_ok"], 2)
        pe.wait_ge(S["slots_ok"], 1)
        over_experts(pe, experts)
        hidden_transposes(NE // 2, -1, NB - 1)
        down(NE // 2, -1, NB - 1)

    @block.scalar
    def _(act):
        def stats(i):
            act.wait_ge(xs_in[i % 2], 16 * (i // 2 + 1))
            for h in (0, 1):
                last = act.activation(bank[6][:, :], xstat[:, i % 2, h * 512:(h + 1) * 512], ACT.Square,
                                      accum_out=stat[:, h, i:i + 1])
                act.drain()
            act.sem_inc(S["xs_used"], 1)

        act.wait_ge(S["cols_ok"], 1)
        for v, c in ((0, C_C), (1, C_CC)):
            last = act.activation(silu_c[:, :, v], cols[:, c:c + DK], ACT.Silu)
        last.then_inc(S["silu_ok"], 1)
        for layer in (0, 1):
            act.wait_ge(S["sin_in"], layer + 1)
            act.activation(fsin[:, layer, :, :], farg[:, :, :], ACT.Sin).then_inc(S["sin_ok"], 1)
        order = rowu[:8] + gatu + rowu[8:]

        def rows_out(n):
            act.wait_ge(S["mod_ps"], n + 1)
            ps = bank[4 + n % 2]
            if order[n] in gatu:
                g, o = gatu.index(order[n]) // 4, (gatu.index(order[n]) % 4) * 256
                last = act.activation(gate_b[:, g, o:o + 256], ps[:, 0:256], ACT.Copy)
                last.then_inc(S["mrow_ok"], 1)
            else:
                last = act.activation(mod_row[:, n % 2, :], ps[0:2, 0:256], ACT.Copy)
                last.then_inc(S["mrow_ok"], 1)

        act.wait_ge(S["h_ok"], 2 * TT + 1)
        act.activation(habs[:, 0, :], hfwd[:, :, :].rearrange("p a b -> p (a b)"), ACT.Abs)
        act.activation(habs[:, 1, :], hbwd[:, :, :].rearrange("p a b -> p (a b)"), ACT.Abs).then_inc(S["habs_ok"], 1)
        act.wait_ge(S["norm_ps"], 1)
        act.wait_ge(S["invn_ok"], 1)
        for n in range(8):
            stats(n)
            rows_out(n)
        for i in range(8, KT):
            stats(i)
        act.sem_inc(S["ssq_ok"], 1)
        act.wait_ge(S["var_ok"], 1)
        act.activation(stat[:, 2, :], stat[:, 1, :], ACT.Sqrt).then_inc(S["sqrt_ok"], 1)
        for n in range(8, MU):
            rows_out(n)

        act.wait_ge(S["kps"], 2 * NCLS)
        for k in range(DK):
            if k % 2 == 0:
                act.wait_ge(S["wqkv_in"], 16 * DK // 2)
            act.activation(wqkv_hi[:, k, :], wqkv[:, k, :], ACT.Copy).then_inc(S["wqkvhi_ok"], 1)

        def modulate1(i, h, par):
            w = 1 if is_ctx(i) else 0
            act.wait_ge(S["xT_ps"], i + 1)
            need(act, "hs_ok", i)
            for k in range(DK):
                last = act.activation(hfull[:, k, :], bank[k // 4][:, (k % 4) * P:(k % 4 + 1) * P], ACT.Identity,
                                      bias=mod_t[:, k, w:w + 1], scale=scale1[:, k, w:w + 1])
            last.then_inc(S["full_ok"], 1)

        def squares(i, h, par):
            act.wait_ge(S["kv_ps"], i + 3)
            need(act, "qvar_ok", i)
            flat = qsq[:, :, :].rearrange("p a b -> p (a b)")
            if not is_ctx(i):
                act.activation(flat[:, 0:QW], bank[2 + par][:, :], ACT.Square)
            act.activation(flat[:, QW:QKW], bank[4 + par][:, 0:QKW - QW], ACT.Square)
            act.activation(v_all[:, bass.ds(i, 1), :], bank[4 + par][:, QKW - QW:QKVW - QW], ACT.Copy
                           ).then_inc(S["sq_ok"], 1)
            act.wait_ge(S["qvar_ok"], i + 1)
            g = slice(NQ, NH) if is_ctx(i) else slice(0, NH)
            act.activation(qst[:, 1, g], qst[:, 0, g], ACT.Sqrt).then_inc(S["qsd_ok"], 1)

        over_tiles(act, modulate1, squares)

        act.wait_ge(S["kv_ps"], KT + 2)
        act.wait_ge(S["qk_ok"], KT)
        act.wait_ge(S["hT_in"], 64 + 32 * TT)

        def split_wh(c):
            for g in range(3):
                act.wait_ge(wh_in[g], c * 16 + 16)
                act.wait_ge(S["proj_ps"], c * 6 + 2 * g + 2)
                act.activation(wh_hi[:, g, :, :], wh[:, g, :, :], ACT.Copy).then_inc(S["whhi_ok"], 1)

        def evacuate(c, ahead):
            for g in range(3):
                act.wait_ge(S["conv_ok"], c * 3 + g + 1)
                for h in (0, 1):
                    n = 2 * g + h
                    act.wait_ge(S["proj_ps"], c * 6 + n + 7)
                    act.activation(pad[:, g, 1 + h * 512:1 + (h + 1) * 512], bank[n][:, :], ACT.Copy
                                   ).then_inc(S["evac_ok"], 1)
                if g == 1:
                    ahead()
            act.wait_ge(S["uT_ps"], c + 1)
            for b in (0, 1):
                last = act.activation(uT[:, 4 * b:4 * b + 4, bass.ts(c, P)],
                                      bank[6 + b][:, :].rearrange("p (a b) -> p a b", b=P), ACT.Copy)
            last.then_inc(S["uT_ok"], 1)

        act.wait_ge(S["proj_ps"], 6)
        over_channels(act, split_wh, evacuate)
        for c in range(HC):
            act.wait_ge(S["z_ps"], c + 1)
            if c == 0:
                act.wait_ge(S["us_ps"], 2 * NCLS)
            if c >= 2:
                act.wait_ge(S["mixhy_ok"], c - 1)
            for z in range(4):
                last = act.activation(zs[:, c % 2, z, :], bank[4 * (c % 2) + z][:, :], ACT.Copy)
            last.then_inc(S["z_ok"], 1)

        act.wait_ge(S["mixhy_ok"], HC)
        for w in (0, 1):
            last = act.activation(ks_hi[:, :, :, w, :], qk_all[:, :, NQ:NH, :], ACT.Copy)
        last.then_inc(S["kshi_ok"], 1)
        for n, (w, kv, a) in enumerate(KROUND):
            act.wait_ge(S["kT_ps"], n + 1)
            z = min(a + 4, KT)
            act.activation((kT_hi, kT_lo)[w][:, kv, a * P:z * P], bank[6 + n % 2][:, 0:(z - a) * P], ACT.Copy
                           ).then_inc(S["kT_ok"], 1)

        def high_q(r):
            for hh in (0, 1):
                act.activation(qs[:, hh, :, 0, :], qk_all[:, 0:TT, bass.ds(r + 4 * hh, 1), :].squeeze(2), ACT.Copy
                               ).then_inc(S["qshi_ok"], 1)

        def queries_out(hh, half, ps):
            return act.activation(qT[:, hh, half * 512:(half + 1) * 512], ps[:, :], ACT.Copy)

        high_q(0)
        for hh in (0, 1):
            act.wait_ge(S["kT_ps"], len(KROUND) + hh + 1)
            queries_out(hh, 0, bank[6 + hh]).then_inc(S["kT_ok"], 1)
        act.wait_ge(S["at_free"], 1)

        def soften(r, kind):
            for s, rounds in enumerate(ROUNDS[kind]):
                for n in range(max(3, len(rounds))):
                    if n == 2 and not (kind == "first" and s == 0) and not (kind == "tail" and s > 0):
                        e = (s - 1) % STEPS
                        act.wait_ge(S["mx_ok"], r * STEPS + s)
                        if not (kind == "first" and s < 5):
                            act.wait_ge(S["t_ps"], r * RB + (thirds_done(kind, s - 5 + LAG) + 1))
                        act.activation(prob[:, e % 4, :], psum[:, 1536 * (e % 2):1536 * (e % 2) + KT * P], ACT.Exp,
                                       bias=nmax[:, e % 4:e % 4 + 1], accum_out=psums[:, e % 4:e % 4 + 1]
                                       ).then_inc(S["p_ok"], 1)
                    if n >= len(rounds):
                        continue
                    k, what = rounds[n][:2]
                    act.wait_ge(S["t_ps"], r * RB + (k + 1))
                    if what == "p":
                        b, (a, z) = (s - LAG) % STEPS, TROUND[n]
                        if b % 8 == 0 and n == 0 and not (kind == "first" and s == LAG):
                            act.wait_ge(S["pv_ps"], r * 2 + b // 8)
                        last = act.activation(probT[:, b // 4 % 2, a:z, (b % 4) * P:(b % 4 + 1) * P],
                                              bank[6 + k % 2][:, 0:(z - a) * P].rearrange("p (a b) -> p a b", b=P),
                                              ACT.Copy)
                    else:
                        last = queries_out(*rounds[n][2:], bank[6 + k % 2])
                    last.then_inc(S["te_ok"], 1)
                if s == 8 and kind != "last":
                    high_q(r + 1)

        over_pairs(act, soften)

        act.wait_ge(S["pve_ok"], 2 * NPAIR)
        for k in range(DK):
            act.wait_ge(wo_in[k % 4], 32 if k < NPAIR else 48)
            act.activation(wo_hi[:, k, :], wo[:, k % 4, :], ACT.Copy).then_inc(S["wohi_ok"], 1)

        def high_mix(i, par):
            need(act, "o_ps", i - 1)
            act.activation(ms_hi[:, par, 0:4, :], mix_at[:, :, bass.ts(i, P)], ACT.Copy)
            act.activation(ms_hi[:, par, 4:8, :], mix_hy[:, :, bass.ts(i, P)], ACT.Copy).then_inc(S["mshi_ok"], 1)

        def ahead_mix(i, h, par):
            if not (isinstance(i, int) and i == TT - 1):
                high_mix(i + 1, 1 - par)

        def second_norm(i, h, par):
            act.wait_ge(S["x1_ok"], i + 1)
            act.activation(junk[:, :], x1[:, par, :], ACT.Square, accum_out=st2[:, 0, par:par + 1]
                           ).then_inc(S["ssq2_ok"], 1)
            act.wait_ge(S["var2_ok"], i + 1)
            act.activation(st2[:, 2, par:par + 1], st2[:, 1, par:par + 1], ACT.Sqrt).then_inc(S["sd2_ok"], 1)
            act.wait_ge(S["x2T_ps"], i + 1)
            need(act, "r_ps", i)
            for k in range(DK):
                last = act.activation(hs2[:, par, k, :], bank[4 + k // 4][:, (k % 4) * P:(k % 4 + 1) * P],
                                      ACT.Identity, bias=mod_t[:, 3 * DK + k, 0:1], scale=scale2[:, k:k + 1])
            last.then_inc(S["hx2_ok"], 1)
            act.wait_ge(S["rmx_ok"], i + 1)
            act.activation(aff_t[:, bass.ds(i, 1), :].squeeze(1), bank[6][:, 0:NE], ACT.Exp,
                           bias=st2[:, 5, par:par + 1], accum_out=st2[:, 6, par:par + 1]).then_inc(S["rexp_ok"], 1)

        act.wait_ge(S["mixhy_ok"], HC)
        high_mix(0, 0)
        over_out(act, ahead_mix, second_norm)
        act.wait_ge(S["affT_ps"], 1)
        for h in (0, 1):
            last = act.activation(aff[:, 0, h * 512:(h + 1) * 512], bank[4 + h][0:NE, :], ACT.Copy)
        last.then_inc(S["affT_ok"], 1)
        def token_out(e, q, ps):
            act.wait_ge(S["xx_ps"], e * 2 + (q + 1))
            need(act, "xe_ok", e)
            for k in range(4):
                kk = 4 * q + k
                last = act.activation(xf[:, kk, :], ps[:, k * P:(k + 1) * P], ACT.Identity,
                                      bias=mod_t[:, 3 * DK + kk, 0:1], scale=scale2[:, kk:kk + 1])
            last.then_inc(S["xf_ok"], 1)

        def high_unit(i, n, b, m):
            u, w = 2 * n + m, width(b)
            act.wait_ge(wraw_in[u % 4], i * (16 * 7) + 16 * (u // 4 + 1))
            need(act, "gu_ps", i * 28 + (u - 1))
            act.activation(we_hi[:, m, :, 0:w], wraw[:, u % 4, :, 0:w], ACT.Copy).then_inc(S["hi_ok"], 1)

        def gate_unit(i, n, b):
            act.wait_ge(S["gu_ps"], i * 28 + (2 * n + 1))
            need(act, "hid_ok", i * 14 + n)
            act.activation(sil[:, 0:width(b)], bank[2 * (n % 2)][:, 0:width(b)], ACT.Silu).then_inc(S["sil_ok"], 1)

        def hidden_out(i, n, b):
            act.wait_ge(S["hidT_ps"], i * 14 + (n + 1))
            need(act, "d_ps", i * 14 + (n - 1))
            full = width(b) // P
            last = act.activation(hidT[:, n % 2, 0:full, :], bank[4 + n % 2][:, 0:full * P].rearrange(
                "p (a b) -> p a b", b=P), ACT.Copy)
            if width(b) % P:
                c = width(b) % P
                last = act.activation(hidT[0:c, n % 2, full, :], bank[4 + n % 2][0:c, full * P:(full + 1) * P], ACT.Copy)
            last.then_inc(S["hidT_ok"], 1)

        def experts(i):
            for n, (ee, b) in enumerate(BLOCKS):
                before = not (isinstance(i, int) and i == 0 and n == 0)
                pb = BLOCKS[n - 1][1]
                high_unit(i, n, b, 0)
                if before:
                    gate_unit(i, n - 1, pb)
                high_unit(i, n, b, 1)
                if b in (3, 4):
                    token_out(i * 2 + (ee + 1), b - 3, bank[4 + (n - 2) % 2])
                if before:
                    hidden_out(i, n - 1, pb)

        act.wait_ge(S["tops_ps"], 1)
        act.wait_ge(S["aff_ok"], TT)
        act.wait_ge(S["slots_ok"], 1)
        for q in (0, 1):
            token_out(0, q, bank[4 + q])
        over_experts(act, experts)
        gate_unit(NE // 2, -1, NB - 1)
        hidden_out(NE // 2, -1, NB - 1)

    def newton(v, y, var, tmp):
        v.tensor_tensor(tmp, y, y, ALU.mult)
        v.drain()
        v.tensor_tensor(tmp, tmp, var, ALU.mult)
        v.drain()
        v.tensor_scalar(tmp, tmp, -0.5, 1.5, ALU.mult, ALU.add)
        v.drain()
        return v.tensor_tensor(y, y, tmp, ALU.mult)

    def parts(v, src, dst):
        s = [src[:, 2 * n2:2 * n2 + 2, :].rearrange("p a b -> p (a b)") for n2 in range(4)]
        d = lambda i: dst[:, i, :]
        v.tensor_tensor(d(VA), s[0], s[2], ALU.add)
        v.tensor_tensor(d(VB), s[1], s[3], ALU.add)
        v.tensor_tensor(d(R2), s[0], s[2], ALU.subtract)
        v.tensor_tensor(d(I2), s[1], s[3], ALU.subtract)
        v.drain()
        v.tensor_tensor(d(V0), d(VA), d(VB), ALU.add)
        v.tensor_tensor(d(V4), d(VA), d(VB), ALU.subtract)
        v.scalar_tensor_tensor(d(R1), d(I2), Q8, s[0], ALU.mult, ALU.add)
        v.scalar_tensor_tensor(d(R3), d(I2), -Q8, s[0], ALU.mult, ALU.add)
        v.scalar_tensor_tensor(d(I1), d(VB), Q8, s[2], ALU.mult, ALU.add)
        return v.scalar_tensor_tensor(d(I3), d(VB), Q8, s[2], ALU.mult, ALU.subtract)

    @block.vector
    def _(v):
        v.memset(ones[:, :], 1.0).then_inc(S["ones_ok"], 1)
        v.wait_ge(S["cols_ps"], 1)
        v.tensor_copy(cols[:, :], bank[7][:, 0:132]).then_inc(S["cols_ok"], 1)
        MAGIC = 12582912.0
        TWO_PI_HI = 6.28125
        TWO_PI_LO = 2 * math.pi - TWO_PI_HI
        v.wait_ge(S["filt_in"], 7 * 16)
        for layer, b in ((0, 0), (1, 2)):
            v.wait_ge(S[("l1_ps", "l2_ps")[layer]], 1)
            if layer:
                v.wait_ge(S["sin_ok"], 1)
            for h in (0, 1):
                v.tensor_scalar(farg[:, h, :], bank[b + h][0:ORD, :], fcol[:, layer:layer + 1], fcol[:, 2:3],
                                ALU.add, ALU.mult)
            v.drain()
            v.tensor_scalar(fk[:, :, :], farg[:, :, :], 1.0 / (2 * math.pi), MAGIC, ALU.mult, ALU.add)
            v.drain()
            v.tensor_scalar(fk[:, :, :], fk[:, :, :], -MAGIC, None, ALU.add)
            v.drain()
            v.scalar_tensor_tensor(farg[:, :, :], fk[:, :, :], -TWO_PI_HI, farg[:, :, :], ALU.mult, ALU.add)
            v.drain()
            v.scalar_tensor_tensor(farg[:, :, :], fk[:, :, :], -TWO_PI_LO, farg[:, :, :], ALU.mult, ALU.add)
            v.drain()
            v.tensor_scalar(farg[:, :, :], farg[:, :, :], 3.1415925, -3.1415925, ALU.min, ALU.max
                            ).then_inc(S["sin_in"], 1)
        v.wait_ge(S["decay_in"], 16)
        for i in range(2 * TT):
            v.wait_ge(S["l3_ps"], i + 1)
            v.tensor_tensor((hfwd, hbwd)[i % 2][:, i // 2, :], bank[i % 4][:, :], decay[:, i // 2, :],
                            ALU.mult).then_inc(S["h_ok"], 1)
        v.drain()
        v.memset(hbwd[0:1, 0, :], 0.0).then_inc(S["h_ok"], 1)
        v.drain()
        v.tensor_tensor(hdif[:, :, :], hfwd[:, :, :], hbwd[:, :, :], ALU.subtract)
        v.wait_ge(S["habs_ok"], 1)
        v.drain()
        v.tensor_tensor(hfwd[:, :, :], hfwd[:, :, :], hbwd[:, :, :], ALU.add)
        v.wait_ge(S["norm_ps"], 1)
        v.reciprocal(invn[:, :], bank[6][:, :]).then_inc(S["invn_ok"], 1)
        v.drain()
        parts(v, hfwd, vsum).then_inc(S["v_ok"], 1)

        def mod_cols(n, m):
            j = (rowu[:8] + gatu + rowu[8:])[n]
            v.wait_ge(S["mtr_ps"], m + 1)
            for w in (0, 1):
                last = v.tensor_tensor(mod_t[:, 2 * j:2 * j + 2, w], bank[7][:, w:4:2],
                                       cols[:, C_BM + 2 * j:C_BM + 2 * j + 2], ALU.add)
            last.then_inc(S["modt_ok"], 1)

        for m in range(8):
            mod_cols(m, m)
        v.drain()
        for w in (0, 1):
            v.scalar_tensor_tensor(scale1[:, :, w], mod_t[:, DK:2 * DK, w], 1.0, cols[:, C_G1:C_G1 + DK],
                                   ALU.add, ALU.mult)
        v.wait_ge(S["silu_ok"], 1)
        v.tensor_copy(silu_b[:, :, :], silu_c[:, :, 0:1].to_broadcast([P, DK, P])).then_inc(S["silub_ok"], 1)
        v.wait_ge(S["ssq_ok"], 1)
        v.drain()
        v.tensor_tensor(stat[:, 0, :], stat[:, 0, :], stat[:, 1, :], ALU.add)
        v.drain()
        v.tensor_scalar(stat[:, 1, :], stat[:, 0, :], 1.0 / DM, EPS, ALU.mult, ALU.add).then_inc(S["var_ok"], 1)
        v.wait_ge(S["sqrt_ok"], 1)
        v.reciprocal(rstd[:, :], stat[:, 2, :])
        v.drain()
        newton(v, rstd[:, :], stat[:, 1, :], stat[:, 0, :]).then_inc(S["mod_done"], 1)
        v.drain()
        parts(v, hdif, vdif).then_inc(S["v_ok"], 1)
        v.drain()
        v.wait_ge(S["bias_in"], 16)
        for i in range(2 * NCLS):
            v.wait_ge(S["kps"], i + 1)
            if i >= 4:
                v.wait_ge(kst[i % 4], 16 * (i // 4))
            last = v.tensor_tensor(kout[:, i % 4, :], bank[i % 4][:, :], invn[:, :], ALU.mult)
            if i == NCLS:
                v.drain()
                v.tensor_tensor(kout[0:1, i % 4, :], kout[0:1, i % 4, :], bias_b[0:1, :], ALU.add
                                ).then_inc(S["kmul"], 1)
            elif i < NCLS:
                last.then_inc(S["kmul"], 1)
                v.drain()
                v.tensor_tensor(kout[:, i % 4, :], kout[:, i % 4, :], bias_b[:, :], ALU.add).then_inc(S["kadd"], 1)
            else:
                last.then_inc(S["kmul"], 1)
        for m in range(8, 16):
            mod_cols(m + 8, m)
        v.drain()
        v.scalar_tensor_tensor(scale2[:, :], mod_t[:, 4 * DK:5 * DK, 0], 1.0, cols[:, C_G2:C_G2 + DK],
                               ALU.add, ALU.mult)
        v.drain()
        v.sem_inc(S["mod_done"], 1)

        for k in range(DK):
            v.wait_ge(S["wqkvhi_ok"], k + 1)
            v.tensor_tensor(wqkv_lo[:, k, :], wqkv[:, k, :], wqkv_hi[:, k, :].bitcast(fp32), ALU.subtract
                            ).then_inc(S["wqkvlo_ok"], 1)
        for i in range(4):
            v.wait_ge(kst[i], 16 * NCLS // 2)
        v.drain()
        v.sem_inc(S["xt_used"], 2)
        v.sem_inc(S["full_ok"], 1)
        v.sem_inc(S["kv_ps"], 2)
        v.sem_inc(S["qn_ok"], 2)
        v.sem_inc(S["hT_in"], 64)

        def normalise(i, h, par):
            v.wait_ge(xt_in[par], h * 16 + 16)
            need(v, "xT_ps", i)
            v.tensor_scalar(xn[:, :], xt[:, par, :], rstd[:, bass.ds(i, 1)], None, ALU.mult).then_inc(S["xn_ok"], 1)
            v.drain()
            v.sem_inc(S["xt_used"], 1)
            v.wait_ge(S["full_ok"], i + 2)
            v.wait_ge(S["kv_ps"], i + 1)
            v.wait_ge(S["hT_in"], i * 32 + 32)
            v.tensor_copy(hs_hi[:, par, :, :], hfull[:, :, :])
            v.drain()
            v.tensor_tensor(hs_lo[:, par, :, :], hfull[:, :, :], hs_hi[:, par, :, :].bitcast(fp32), ALU.subtract
                            ).then_inc(S["hs_ok"], 1)

        def head_norm(i, h, par):
            g = slice(NQ, NH) if is_ctx(i) else slice(0, NH)
            v.wait_ge(S["sq_ok"], i + 1)
            v.tensor_reduce(qst[:, 3, g], qsq[:, g, :], AX.X, ALU.add)
            v.drain()
            v.tensor_scalar(qst[:, 0, g], qst[:, 3, g], 1.0 / HD, EPS, ALU.mult, ALU.add).then_inc(S["qvar_ok"], 1)
            v.wait_ge(S["qsd_ok"], i + 1)
            v.reciprocal(qst[:, 2, g], qst[:, 1, g])
            v.drain()
            newton(v, qst[:, 2, g], qst[:, 0, g], qst[:, 3, g])
            v.drain()
            need(v, "qk_ok", i)
            if not is_ctx(i):
                v.tensor_tensor(qn[:, 0:NQ, :], bank[2 + par][:, :].rearrange("p (a b) -> p a b", b=HD),
                                qst[:, 2, 0:NQ].unsqueeze(2).to_broadcast([P, NQ, HD]), ALU.mult)
            v.tensor_tensor(qn[:, NQ:NH, :], bank[4 + par][:, 0:QKW - QW].rearrange("p (a b) -> p a b", b=HD),
                            qst[:, 2, NQ:NH].unsqueeze(2).to_broadcast([P, NKV, HD]), ALU.mult
                            ).then_inc(S["qn_ok"], 1)

        over_tiles(v, normalise, head_norm)

        v.wait_ge(S["qk_ok"], KT)
        v.wait_ge(S["kv_ps"], KT + 2)
        v.wait_ge(S["hT_in"], 64 + 32 * TT)
        v.drain()
        v.memset(pad[:, :, 0:1], 0.0)
        v.memset(pad[:, :, SEQ + 1:SEQ + 2], 0.0)
        v.drain()
        v.sem_inc(S["wh_ok"], 3)
        v.sem_inc(S["evac_ok"], 6)
        v.sem_inc(S["conv_ok"], 3)
        v.sem_inc(S["uT_ok"], 1)
        v.sem_inc(S["proj_ps"], 6)

        def low_wh(c):
            for g in range(3):
                v.wait_ge(S["whhi_ok"], c * 3 + g + 1)
                v.tensor_tensor(wh_lo[:, g, :, :], wh[:, g, :, :], wh_hi[:, g, :, :].bitcast(fp32), ALU.subtract
                                ).then_inc(S["wh_ok"], 1)

        def convolve(c, ahead):
            for g in range(3):
                v.wait_ge(S["evac_ok"], c * 6 + 2 * g + 8)
                w = [cols[:, bass.ds(c + (C_CW + tap * 12 + GROUP[g] * HC), 1)] for tap in range(3)]
                b = cols[:, bass.ds(c + (C_CB + GROUP[g] * HC), 1)]
                if g == 1:
                    need(v, "uT_ps", c)
                dst = (vconv[:, :], gated[:, :], x2_all[:, bass.ds(c, 1), :].squeeze(1))[g]
                v.tensor_scalar(dst, pad[:, g, 1:SEQ + 1], w[1], b, ALU.mult, ALU.add)
                v.drain()
                v.scalar_tensor_tensor(dst, pad[:, g, 0:SEQ], w[0], dst, ALU.mult, ALU.add)
                v.drain()
                last = v.scalar_tensor_tensor(dst, pad[:, g, 2:SEQ + 2], w[2], dst, ALU.mult, ALU.add)
                last.then_inc(S["conv_ok"], 1)
                if g == 1:
                    v.drain()
                    v.tensor_tensor(gated[:, :], gated[:, :], vconv[:, :], ALU.mult).then_inc(S["u_ok"], 1)
                    ahead()
            v.drain()
            v.sem_inc(S["x2_ok"], 1)

        over_channels(v, low_wh, convolve)
        v.wait_ge(S["uT_ok"], HC + 1)
        v.wait_ge(S["proj_ps"], 6 * HC + 6)
        v.drain()
        parts(v, uT, vu).then_inc(S["vu_ok"], 1)
        for i in range(NCLS):
            b = 2 * (i % 4)
            v.wait_ge(kin_in[i % 2], 32 * (i // 2 + 1))
            if i >= 2:
                v.wait_ge(S["y_ok"], i - 1)
            v.wait_ge(S["us_ps"], 2 * i + 2)
            kr, kn = kin[:, i % 2, 0, :], kin[:, i % 2, 1, :]
            for n, (u, k) in enumerate(((b, kr), (b + 1, kn), (b, kn), (b + 1, kr))):
                last = v.tensor_tensor(prod[:, i % 2, n, :], bank[u][:, :], k, ALU.mult)
            last.then_inc(S["prod_ok"], 1)
        v.wait_ge(S["y_ok"], NCLS)
        for c in range(HC):
            v.wait_ge(S["z_ok"], c + 1)
            zr = [zs[:, c % 2, z, 0:N1] for z in range(4)]
            zi = [zs[:, c % 2, z, N1:512] for z in range(4)]
            A, B, E, D, F, G, DF, SF = [ztmp[:, n, :] for n in range(8)]
            y = [ysum[:, n, :] for n in range(4)]
            for dst, p0, p1, op in ((A, zr[0], zi[0], ALU.add), (B, zr[0], zi[0], ALU.subtract),
                                    (E, zr[1], zr[3], ALU.add), (D, zr[1], zr[3], ALU.subtract),
                                    (F, zi[1], zi[3], ALU.add), (G, zi[3], zi[1], ALU.subtract)):
                v.tensor_tensor(dst, p0, p1, op)
            v.drain()
            for dst, p0, p1, op in ((y[0], A, zr[2], ALU.add), (y[2], A, zr[2], ALU.subtract),
                                    (y[1], B, zi[2], ALU.subtract), (y[3], B, zi[2], ALU.add),
                                    (DF, D, F, ALU.subtract), (SF, D, F, ALU.add)):
                v.tensor_tensor(dst, p0, p1, op)
            v.drain()
            v.tensor_tensor(y[0], y[0], E, ALU.add)
            v.tensor_tensor(y[2], y[2], G, ALU.add)
            v.scalar_tensor_tensor(y[1], DF, Q8, y[1], ALU.mult, ALU.add)
            v.scalar_tensor_tensor(y[3], SF, -Q8, y[3], ALU.mult, ALU.add)
            v.drain()
            v.tensor_tensor(mix_hy[:, c, :], ysum[:, :, :].rearrange("p a b -> p (a b)"), x2_all[:, c, :], ALU.mult
                            ).then_inc(S["mixhy_ok"], 1)

        v.wait_ge(S["kshi_ok"], 1)
        v.drain()
        for w in (0, 1):
            last = v.tensor_tensor(ks_lo[:, :, :, w, :], qk_all[:, :, NQ:NH, :], ks_hi[:, :, :, w, :].bitcast(fp32),
                                   ALU.subtract)
        last.then_inc(S["kslo_ok"], 1)
        v.sem_inc(S["te_ok"], 3 * LAG)
        v.sem_inc(S["t_ps"], 3 * LAG)
        v.sem_inc(S["p_ok"], 2)
        v.sem_inc(S["at_free"], 1)

        def low_q(r):
            for hh in (0, 1):
                v.wait_ge(S["qshi_ok"], r * 2 + hh + 1)
                v.tensor_tensor(qs[:, hh, :, 1, :], qk_all[:, 0:TT, bass.ds(r + 4 * hh, 1), :].squeeze(2),
                                qs[:, hh, :, 0, :].bitcast(fp32), ALU.subtract).then_inc(S["qslo_ok"], 1)

        def maxima(r, kind):
            for s in range(len(ROUNDS[kind])):
                if kind != "tail":
                    v.wait_ge(S["s_ps"], r * STEPS + s + 1)
                    v.tensor_reduce(nmax[:, s % 4:s % 4 + 1], psum[:, 1536 * (s % 2):1536 * (s % 2) + KT * P], AX.X,
                                    ALU.max, negate=True).then_inc(S["mx_ok"], 1)
                if not (kind == "first" and s == 0) and not (kind == "tail" and s > 0):
                    v.wait_ge(S["p_ok"], r * STEPS + s + 2)
                    v.reciprocal(prcp[:, (s - 1) % 4:(s - 1) % 4 + 1], psums[:, (s - 1) % 4:(s - 1) % 4 + 1]
                                 ).then_inc(S["rs_ok"], 1)
                if s == V_SLOT[1] or (s == V_SLOT[0] and kind != "first"):
                    pair, half = (r, 0) if s > 8 else (r - 1, 1)
                    v.wait_ge(S["pv_ps"], r * 2 + (s > 8))
                    v.tensor_copy(mix_at[:, bass.ds(pair, 1), half * 512:(half + 1) * 512].squeeze(1), bank[V_BANK][:, :]
                                  ).then_inc(S["pve_ok"], 1)
                if s == 9 and kind != "last":
                    low_q(r + 1)

        low_q(0)
        over_pairs(v, maxima)

        for k in range(DK):
            v.wait_ge(S["wohi_ok"], k + 1)
            v.tensor_tensor(wo_lo[:, k, :], wo[:, k % 4, :], wo_hi[:, k, :].bitcast(fp32), ALU.subtract
                            ).then_inc(S["wo_ok"], 1)

        def low_mix(i, par):
            v.wait_ge(S["mshi_ok"], i + 1)
            v.tensor_tensor(ms_lo[:, par, 0:4, :], mix_at[:, :, bass.ts(i, P)], ms_hi[:, par, 0:4, :].bitcast(fp32),
                            ALU.subtract)
            v.tensor_tensor(ms_lo[:, par, 4:8, :], mix_hy[:, :, bass.ts(i, P)], ms_hi[:, par, 4:8, :].bitcast(fp32),
                            ALU.subtract).then_inc(S["ms_ok"], 1)

        def ahead_low(i, h, par):
            if not (isinstance(i, int) and i == TT - 1):
                low_mix(i + 1, 1 - par)

        def residual_and_route(i, h, par):
            c = lambda n: st2[:, n, par:par + 1]
            v.wait_ge(xr_in[par], h * 16 + 16)
            v.wait_ge(S["o_ps"], i + 1)
            v.wait_ge(xst[par], h * 32 + 32)
            for half in (0, 1):
                v.tensor_tensor(gmix[:, half * 512:(half + 1) * 512], bank[2 * par + half][:, :],
                                gate_b[:, 0, half * 512:(half + 1) * 512], ALU.mult)
            v.drain()
            v.tensor_tensor(x1[:, par, :], gmix[:, :], xr[:, par, :], ALU.add).then_inc(S["x1_ok"], 1)
            v.wait_ge(S["ssq2_ok"], i + 1)
            v.tensor_scalar(c(1), c(0), 1.0 / DM, EPS, ALU.mult, ALU.add).then_inc(S["var2_ok"], 1)
            v.wait_ge(S["sd2_ok"], i + 1)
            v.reciprocal(c(3), c(2))
            v.drain()
            newton(v, c(3), c(1), c(4))
            v.drain()
            need(v, "x2T_ps", i)
            v.tensor_scalar(xn2[:, par, :], x1[:, par, :], c(3), None, ALU.mult).then_inc(S["xn2_ok"], 1)
            v.wait_ge(S["r_ps"], i + 1)
            v.tensor_reduce(c(5), bank[6][:, 0:NE], AX.X, ALU.max, negate=True).then_inc(S["rmx_ok"], 1)
            v.wait_ge(S["rexp_ok"], i + 1)
            v.reciprocal(c(7), c(6))
            v.drain()
            a = aff_t[:, bass.ds(i, 1), :].squeeze(1)
            v.tensor_scalar(a, a, c(7), None, ALU.mult).then_inc(S["aff_ok"], 1)

        for par in (0, 1):
            v.sem_inc(xst[par], 32)
        low_mix(0, 0)
        over_out(v, ahead_low, residual_and_route)
        v.wait_ge(S["affT_ok"], 1)
        for r in range(CAP // 8):
            src, dst = aff[:, r % 2, :], aff[:, 1 - r % 2, :]
            best = top_v[:, 8 * r:8 * r + 8]
            v.max(best, src)
            v.drain()
            v.max_index(top_i[:, 8 * r:8 * r + 8], best, src)
            if r < CAP // 8 - 1:
                v.match_replace(dst, best, src, -1.0)
            v.drain()
        v.tensor_copy(top_f[:, :], top_i[:, :]).then_inc(S["top_ok"], 1)
        v.wait_ge(S["tops_ps"], 1)
        v.tensor_copy(slot_i[:, 0:NE], bank[6][:, 0:NE])
        v.tensor_copy(slot_i[:, NE:NE + 1], bank[6][:, 0:1])
        v.tensor_copy(slot_g[:, :], bank[6][:, NE:2 * NE]).then_inc(S["slots_ok"], 1)
        def split_tokens(e, slot):
            v.wait_ge(S["xf_ok"], e * 2 + 2)
            v.tensor_copy(xe_hi[:, slot, :, :], xf[:, :, :])
            v.drain()
            v.tensor_tensor(xe_lo[:, slot, :, :], xf[:, :, :], xe_hi[:, slot, :, :].bitcast(fp32), ALU.subtract
                            ).then_inc(S["xe_ok"], 1)

        def low_unit(i, n, b, m):
            u, w = 2 * n + m, width(b)
            v.wait_ge(S["hi_ok"], i * 28 + (u + 1))
            v.tensor_tensor(we_lo[:, m, :, 0:w], wraw[:, u % 4, :, 0:w], we_hi[:, m, :, 0:w].bitcast(fp32),
                            ALU.subtract).then_inc(S["lo_ok"], 1)

        def hidden(i, n, b):
            w = width(b)
            v.wait_ge(S["sil_ok"], i * 14 + (n + 1))
            v.wait_ge(S["gu_ps"], i * 28 + (2 * n + 2))
            need(v, "hidT_ps", i * 14 + (n - 1))
            v.tensor_tensor(hid[:, n % 2, 0:w], sil[:, 0:w], bank[2 * (n % 2) + 1][:, 0:w], ALU.mult
                            ).then_inc(S["hid_ok"], 1)

        def result(e):
            v.wait_ge(S["d_ps"], e * NB + NB)
            need(v, "scat", e * 16)
            for half in (0, 1):
                cs = slice(half * 512, (half + 1) * 512)
                last = v.scalar_tensor_tensor(yb[:, cs], bank[6 + half][:, :], slot_g[:, bass.ds(e, 1)],
                                              gate_b[:, 1, cs], ALU.mult, ALU.mult)
            last.then_inc(S["ye_ok"], 1)

        def experts(i):
            for n, (ee, b) in enumerate(BLOCKS):
                before = not (isinstance(i, int) and i == 0 and n == 0)
                low_unit(i, n, b, 0)
                if before:
                    hidden(i, n - 1, BLOCKS[n - 1][1])
                low_unit(i, n, b, 1)
                if b == 1 and not (isinstance(i, int) and i == 0 and ee == 0):
                    result(i * 2 + (ee - 1))
                if b == 5:
                    split_tokens(i * 2 + (ee + 1), 1 - ee)

        v.drain()
        split_tokens(0, 0)
        over_experts(v, experts)
        hidden(NE // 2, -1, NB - 1)
        result(NE - 1)

    ctx.close()


_DRAWN = """x c ctx c_ctx w_mod b_mod norm1_g norm2_g w_in w_out q_norm_g k_norm_g conv_w conv_b filt_w1 filt_b1
    filt_w2 filt_b2 filt_w3 filt_freq hyena_bias w_router w_gate w_up w_down""".split()


def kernel(**inputs):
    import numpy as np
    import concourse.bacc as bacc
    from concourse.bass_utils import run_bass_kernel_spmd as run

    nc = bacc.Bacc("TRN2", target_bir_lowering=False, num_devices=1)
    arrays, aps = {}, {}
    given = {n: np.ascontiguousarray(inputs[n]) for n in _DRAWN}
    given.update(constants())
    for name, a in given.items():
        arrays["in_" + name] = a
        aps[name] = nc.dram_tensor("in_" + name, a.shape, mybir.dt.from_np(a.dtype), kind="ExternalInput").ap()
    out = nc.dram_tensor("out", [1, SEQ, DM], mybir.dt.float32, kind="ExternalOutput").ap()
    build(nc, aps, out)
    r = run(nc, [arrays], core_ids=[0])
    return r.results[0]["out"]
```

```python
import math
from contextlib import ExitStack

import concourse.bass as bass
from concourse import mybir

P = 128
DM = 1024
SEQ = 1024
CTX = 256
DK = DM // P
TT = SEQ // P
CT = CTX // P
KT = TT + CT
HD = 64
NQ = 8
NKV = 2
NH = NQ + NKV
QW = NQ * HD
QKW = NH * HD
QKVW = QKW + NKV * HD
HYW = 512
HC = HYW // P
GRID_W = 64
EMB = 33
ORD = 64
NE = 16
CAP = 2 * SEQ // NE
FF = 2752
EPS = 1e-6
NFFT = 2 * SEQ
N1 = NFFT // 8
NCLS = 8
FW0 = 5 * P
FW = FW0 + 3 * 3 * N1
IV = 4 * N1
Q8 = math.sqrt(0.5)


def constants():
    import numpy as np
    f32 = np.float32
    n1 = np.arange(N1)
    th = 2 * np.pi / NFFT

    def ang(k2, k1):
        return th * (np.outer(n1, k2 + 8 * k1) % NFFT)
    fwd, inv = [], []
    j = np.arange(P)
    a0, a4 = ang(0, j), ang(4, j)
    nyq = np.zeros((N1, P))
    nyq[:, 0] = np.where(n1 % 2, -1.0, 1.0)
    for m in (np.cos(a0), np.sin(a0), nyq, np.cos(a4), np.sin(a4)):
        fwd.append(m)
    for k2 in (1, 2, 3):
        a = ang(k2, np.arange(N1))
        fwd += [np.cos(a), np.sin(a), -np.sin(a)]
    fwd = np.concatenate(fwd, 1).reshape(2, P, -1).transpose(1, 0, 2)
    w0 = np.full((P, 1), 2.0 / NFFT)
    w0[0] = 1.0 / NFFT
    c0, s0 = np.cos(a0).T * w0, np.sin(a0).T * w0
    s0[0] = nyq[:, 0] / NFFT
    inv += [c0, s0, np.cos(a4).T * 2 / NFFT, np.sin(a4).T * 2 / NFFT]
    for k2 in (1, 2, 3):
        a = ang(k2, np.arange(N1)).T * 1.0
        c, s = np.cos(a) * 2 / NFFT, np.sin(a) * 2 / NFFT
        for t in (0, 1):
            r = slice(t * P, t * P + P)
            inv += [np.concatenate([c[r], s[r]], 1), np.concatenate([s[r], -c[r]], 1)]
    inv = np.concatenate(inv, 1)
    t = np.linspace(0.0, 1.0, SEQ, dtype=f32)[:, None]
    bands = (EMB - 1) // 2
    w = f32(2.0 * math.pi) * np.arange(SEQ, dtype=f32) / f32(SEQ)
    f = np.linspace(1e-4, bands - 1, bands, dtype=f32)
    fw = w[:, None] * f[None, :]
    z = np.concatenate([t, np.cos(fw), -np.sin(fw)], -1).T
    dmax, dmin = math.log(1e-2) / 0.3, math.log(1e-2) / 1.5
    deltas = np.linspace(dmin, dmax, HYW, dtype=f32)
    decay = np.exp(-t * np.abs(deltas))
    quarter = HD // 4
    invf = (f32(10000.0) ** (-np.arange(quarter, dtype=f32) / f32(quarter))).astype(f32)
    tok = np.arange(SEQ)
    pos = np.stack([tok // GRID_W, tok % GRID_W], -1).astype(f32)
    an = pos[..., None] * invf
    rope = np.stack([np.cos(an), np.sin(an)], 1)
    return {
        "fwd": np.ascontiguousarray(fwd, f32), "inv": np.ascontiguousarray(inv, f32),
        "feat": np.ascontiguousarray(z, f32), "decay": np.ascontiguousarray(decay, f32),
        "rope": np.ascontiguousarray(rope.reshape(SEQ, 64), f32), "ident": np.eye(P, dtype=f32),
        "flip": np.ascontiguousarray(np.eye(P, dtype=f32)[::-1]),
    }


def build(nc, t, out):
    fp32, fp32r = mybir.dt.float32, mybir.dt.float32r
    i32, u32 = mybir.dt.int32, mybir.dt.uint32
    ALU, ACT, AX = mybir.AluOpType, mybir.ActivationFunctionType, mybir.AxisListType
    ctx = ExitStack()

    def sem(name):
        return ctx.enter_context(nc.semaphore(name))

    def at(name, shape, kb, dt=fp32):
        return nc.alloc_sbuf_tensor_at(name, shape, dt, offset=int(kb * 1024) - 896)

    psum = ctx.enter_context(nc.psum_tensor("psum", [P, 8 * 512], fp32))
    bank = [psum[:, i * 512:(i + 1) * 512] for i in range(8)]

    kscr = nc.dram_tensor("kscr", [2, NCLS, P, HYW], fp32, kind="Internal").ap()

    ident = at("ident", [P, P], 17)
    cols = at("cols", [P, 132], 17.5)
    C_C, C_CC, C_G1, C_G2, C_BM, C_CW, C_CB = 0, 8, 16, 24, 32, 80, 116
    silu_c = at("silu_c", [P, DK, 2], 18.125)
    mod_t = at("mod_t", [P, 6 * DK, 2], 18.25)
    scale1 = at("scale1", [P, DK, 2], 18.75)
    scale2 = at("scale2", [P, DK], 18.875)
    rstd = at("rstd", [P, KT], 19)
    stat = at("stat", [P, 3, KT], 19.0625)
    ones = at("ones", [P, P], 19.25)
    silu_b = at("silu_b", [P, DK, P], 28)
    gate_b = at("gate_b", [P, 2, DM], 32)
    decay = at("decay", [P, TT, HYW], 40)
    hdif = at("hdif", [P, TT, HYW], 40)
    hfwd = at("hfwd", [P, TT, HYW], 56)
    hbwd = at("hbwd", [P, TT, HYW], 72)
    vsum = at("vsum", [P, 10, 2 * HYW], 88)
    vdif = at("vdif", [P, 10, 2 * HYW], 128)
    habs = at("habs", [P, 2, TT * HYW], 128)
    rows1 = at("rows1", [80, P], 88)
    rows2 = at("rows2", [52, P], 88.5)
    feat = at("feat", [EMB, SEQ], 89)
    fw1 = at("fw1", [EMB, ORD], 93)
    fw2 = at("fw2", [ORD, ORD], 93.25)
    fcol = at("fcol", [ORD, 3], 93.5)
    fw3 = at("fw3", [ORD, 2 * HYW], 94)
    farg = at("farg", [ORD, 2, 512], 98)
    fk = at("fk", [ORD, 2, 512], 102)
    fsin = at("fsin", [ORD, 2, 2, 512], 106)
    fwd = at("fwd", [P, 2, FW], 168)
    kout = at("kout", [P, 4, HYW], 192)
    kout2 = at("kout2", [P, 4, HYW], 100)
    xstat = at("xstat", [P, 2, DM], 192)
    invn = at("invn", [P, HYW], 22)
    bias_b = at("bias_b", [P, HYW], 24)
    mod_row = at("mod_row", [2, 2, 256], 26)
    kslot = lambda n: (kout, kout2)[n // NCLS][:, n % 4, :]
    wmod = at("wmod", [P, 3, DK, 256], 200)

    names = """ident_in rows_in filt_in decay_in fwd_in bias_in brow_in cols_ps cols_ok silu_ok silub_ok
        l1_ps l2_ps sin_in sin_ok l3_ps h_ok habs_ok habs_sum norm_ps invn_ok v_ok kps kmul kadd
        mod_ps mrow_ok mtr_ps xs_used ssq_ok sqrt_ok var_ok ones_ok""".split()
    S = {n: sem(n) for n in names}
    wm_in = [sem(f"wm_in{i}") for i in range(3)]
    xs_in = [sem(f"xs_in{i}") for i in range(2)]
    kst = [sem(f"kst{i}") for i in range(4)]
    MU = 6 * DM // 256
    rowu = [j for j in range(MU) if j * 256 // DM not in (2, 5)]
    gatu = [j for j in range(MU) if j * 256 // DM in (2, 5)]

    order = rowu + gatu
    STAT0 = 10

    C0, S0, NY, C4, S4 = 0, 128, 256, 384, 512
    V0, V4, R1, I1, R2, I2, R3, I3, VA, VB = range(10)
    STAGE = (1, 2, 4, 4, 4, 4, 5, 5)

    def terms(side):
        out = []
        out.append([(C0, V0, 0)] if side == 0 else [(S0, V0, 0), (NY, V0, 1)])
        out.append([(C4, V4, 0)] if side == 0 else [(S4, V4, 0)])
        for k2 in (1, 2, 3):
            base = FW0 + (k2 - 1) * 3 * N1
            r, i = 2 * k2, 2 * k2 + 1
            for h in (0, 128):
                out.append([(base + h, r, 0), (base + 512 + h, i, 0)] if side == 0
                           else [(base + h, i, 0), (base + 256 + h, r, 0)])
        return out

    def transform(pe, psum, side, tile, v, vnyq, fm):
        mm = [(c, w, vnyq if ny else v, j) for c, w, ny in terms(side)[tile] for j in (0, 1)]
        for n, (c, w, src, j) in enumerate(mm):
            last = pe.matmul(psum[:, :], fm[:, j, c:c + P], src[:, w, j * HYW:(j + 1) * HYW],
                             start=(n == 0), stop=(n == len(mm) - 1))
        return last

    def mod_unit(pe, n, j):
        pe.wait_ge(wm_in[n % 3], 16 * (n // 3 + 1))
        gate = j in gatu
        ps = bank[4 + n % 2]
        if n >= 2:
            pe.wait_ge(S["mrow_ok"], n - 1)
        for k in range(DK):
            lhs = silu_b[:, k, :] if gate else silu_c[:, k, :]
            last = pe.matmul(ps[0:P if gate else 2, 0:256], lhs, wmod[:, n % 3, k, :],
                             start=(k == 0), stop=(k == DK - 1) and not gate)
        if gate:
            g, o = gatu.index(j) // 4, (gatu.index(j) % 4) * 256
            pe.matmul(ps[:, 0:256], ones[0:1, :], gate_b[0:1, g, o:o + 256],
                      start=False, stop=True).then_inc(S["mod_ps"], 1)
        else:
            last.then_inc(S["mod_ps"], 1)
        return gate

    qk_all = at("qk_all", [P, KT, NH, HD], 88)
    v_all = at("v_all", [P, KT, NKV * HD], 113)
    wqkv_hi = at("wqkv_hi", [P, DK, QKVW], 40, fp32r)
    wqkv_lo = at("wqkv_lo", [P, DK, QKVW], 64, fp32r)
    xt = at("xt", [P, 2, DM], 118)
    rtmp = at("rtmp", [P, 2, NH * HD // 2], 126)
    head_g = at("head_g", [P, 2, HD], 198)
    hT_hi = at("hT_hi", [P, DK, SEQ], 130, fp32r)
    hT_lo = at("hT_lo", [P, DK, SEQ], 162, fp32r)
    xn = at("xn", [P, DM], 194)
    wqkv = at("wqkv", [P, DK, QKVW], 200)
    hs_hi = at("hs_hi", [P, 2, DK, P], 200, fp32r)
    hs_lo = at("hs_lo", [P, 2, DK, P], 208, fp32r)
    hfull = at("hfull", [P, DK, P], 216)
    qsq = at("qsq", [P, NH, HD], 220)
    rope = at("rope", [P, TT, 2, 2, HD // 4], 20)
    qn = at("qn", [P, NH, HD], 26)
    qst = at("qst", [P, 4, NH], 222.5)
    names1 = """wqkv_in wqkvhi_ok wqkvlo_ok small1_in xt_used xn_ok xT_ps full_ok hs_ok hT_in kv_ps sq_ok
        qvar_ok qsd_ok qn_ok qk_ok""".split()
    S.update({n: sem(n) for n in names1})
    xt_in = [sem(f"xt_in{i}") for i in range(2)]

    def need(eng, name, value):
        if not (isinstance(value, int) and value <= 0):
            eng.wait_ge(S[name], value)

    def over_tiles(eng, first, second):
        first(0, 0, 0)
        first(1, 0, 1)
        second(0, 0, 0)
        with eng.Fori(1, TT // 2) as i:
            first(i * 2, i, 0)
            second(i * 2 - 1, i - 1, 1)
            first(i * 2 + 1, i, 1)
            second(i * 2, i, 0)
        for t in range(TT, KT):
            first(t, t // 2, t % 2)
            second(t - 1, (t - 1) // 2, (t - 1) % 2)
        second(KT - 1, (KT - 1) // 2, (KT - 1) % 2)

    def is_ctx(t):
        return isinstance(t, int) and t >= TT

    def split3(pe, ps, hi, lo, w_hi, w_lo, first, last):
        pe.matmul(ps, hi, w_hi, start=first, stop=False)
        pe.matmul(ps, hi, w_lo, start=False, stop=False)
        return pe.matmul(ps, lo, w_hi, start=False, stop=last)

    x2_all = at("x2_all", [P, HC, SEQ], 40)
    uT = at("uT", [P, TT, HYW], 56)
    wh = [at(f"wh{g}", [P, DK, P], kb) for g, kb in ((0, 22), (1, 72), (2, 76))]
    wh_hi = at("wh_hi", [P, 3, DK, P], 118, fp32r)
    wh_lo = at("wh_lo", [P, 3, DK, P], 194, fp32r)
    pad = at("pad", [P, 3, SEQ + 2], 206)
    gated = at("gated", [P, SEQ], 218.5)
    vconv = at("vconv", [P, SEQ], 28)
    vu = at("vu", [P, 10, 2 * HYW], 119)
    fwd3 = at("fwd3", [P, 2, FW], 159)
    yspec = at("yspec", [P, NCLS, 2, HYW], 182)
    kin = at("kin", [P, 2, 2, HYW], 214)
    prod = at("prod", [P, 2, 4, HYW], 72)
    inv_a = at("inv_a", [P, IV + 8 * N1], 20)
    inv_b = at("inv_b", [P, 16 * N1], 56)
    zs = at("zs", [P, 2, 4, 512], 159)
    ztmp = at("ztmp", [P, 8, N1], 214)
    ysum = at("ysum", [P, 4, N1], 175)
    mix_hy = at("mix_hy", [P, HC, SEQ], 72)
    names2 = """proj_ps evac_ok whhi_ok wh_ok conv_ok u_ok uT_ps uT_ok x2_ok vu_ok us_ps prod_ok y_ok
        inv_in z_ps z_ok mixhy_ok fwd3_in fwd3b_in""".split()
    S.update({n: sem(n) for n in names2})
    wh_in = [sem(f"wh_in{i}") for i in range(3)]
    kin_in = [sem(f"kin_in{i}") for i in range(2)]
    GROUP = (2, 0, 1)

    def over_channels(eng, split, work):
        split(0)
        work(0, lambda: split(1))
        with eng.Fori(1, HC - 1) as c:
            work(c, lambda: split(c + 1))
        work(HC - 1, lambda: None)

    mix_at = at("mix_at", [P, NQ // 2, SEQ], 40)
    kT_hi = at("kT_hi", [P, NKV, KT * P], 119, fp32r)
    kT_lo = at("kT_lo", [P, NKV, KT * P], 129, fp32r)
    ks_hi = at("ks_hi", [P, KT, NKV, 2, HD], 139, fp32r)
    ks_lo = at("ks_lo", [P, KT, NKV, 2, HD], 149, fp32r)
    qs = at("qs", [P, 2, TT, 2, HD], 56, fp32r)
    qT = at("qT", [P, 2, SEQ], 64, fp32r)
    prob = at("prob", [P, 4, KT * P], 159)
    probT = at("probT", [P, 2, KT, 512], 179)
    nmax = at("nmax", [P, 4], 219)
    psums = at("psums", [P, 4], 219.125)
    prcp = at("prcp", [P, 4], 219.25)
    names3 = """kshi_ok kslo_ok kT_ps kT_ok qshi_ok qslo_ok s_ps mx_ok p_ok rs_ok pn_ok t_ps te_ok td_ok
        pv_ps pve_ok at_free""".split()
    S.update({n: sem(n) for n in names3})
    STEPS = 16
    NPAIR = NQ // 2
    LAG = 4
    KROUND = [(w, kv, a) for w in (0, 1) for kv in range(NKV) for a in (0, 4, 8)]
    SET = 3 * 512
    TROUND = ((0, 4), (4, 8), (8, KT))
    V_SLOT = (LAG - 1, LAG + 7)
    V_BANK = 3 * (LAG % 2)

    QROUND = {3: (0, 1), 5: (1, 1), 12: (0, 0), 14: (1, 0)}

    def schedule(kind):
        rounds, k = [], -2 if kind == "tail" else 0
        for s in range(LAG if kind == "tail" else STEPS):
            now = []
            for j in range(3):
                if not (kind == "first" and s < LAG):
                    now.append((k, "p", j))
                k += 1
            if kind != "tail" and s in QROUND and not (kind == "last" and s > 8):
                now.append((k, "q") + QROUND[s])
                k += 1
            rounds.append(now)
        return rounds

    ROUNDS = {kind: schedule(kind) for kind in ("first", "mid", "last", "tail")}
    RB = ROUNDS["mid"][-1][-1][0] + 1
    BEFORE = {"mid": "mid", "last": "mid", "tail": "last"}

    def evacuations(kind):
        of, a, d = {}, (-2 if kind == "tail" else 0), 0
        for s, now in enumerate(ROUNDS[kind]):
            if kind == "first" and s < LAG:
                a, d = a + 2, d + 1
            for entry in now:
                if entry[1:] == ("p", 2):
                    d += 1
                    of[entry[0]] = ("td_ok", STEPS, d)
                else:
                    a += 1
                    of[entry[0]] = ("te_ok", RB - STEPS, a)
        return of

    EVACUATED = {kind: evacuations(kind) for kind in ROUNDS}

    def copied(eng, r, kind, k):
        if k in EVACUATED[kind]:
            name, per, count = EVACUATED[kind][k]
            eng.wait_ge(S[name], r * per + count)
        elif kind != "first":
            name, per, count = EVACUATED[BEFORE[kind]][k + RB]
            eng.wait_ge(S[name], r * per + (count - per))

    def thirds_done(kind, s):
        if s < 0:
            return thirds_done(BEFORE[kind], s + STEPS) - RB
        return [r[0] for r in ROUNDS[kind][s] if r[1] == "p"][-1]

    def over_pairs(eng, body):
        body(0, "first")
        with eng.Fori(1, NPAIR - 1) as r:
            body(r, "mid")
        body(NPAIR - 1, "last")
        body(NPAIR, "tail")

    wo_hi = at("wo_hi", [P, DK, DM], 159, fp32r)
    wo_lo = at("wo_lo", [P, DK, DM], 191, fp32r)
    wo = at("wo", [P, 4, DM], 139)
    ms_hi = at("ms_hi", [P, 2, DK, P], 88, fp32r)
    ms_lo = at("ms_lo", [P, 2, DK, P], 96, fp32r)
    xr = at("xr", [P, 2, DM], 104)
    x1 = at("x1", [P, 2, DM], 119)
    xn2 = at("xn2", [P, 2, DM], 127)
    junk = at("junk", [P, DM], 68)
    gmix = at("gmix", [P, DM], 64)
    hs2 = at("hs2", [P, 2, DK, P], 56)
    aff = at("aff", [2 * NE, 2, SEQ // 2], 193)
    top_v = at("top_v", [2 * NE, CAP], 26)
    top_i = at("top_i", [2 * NE, CAP], 26.5, u32)
    top_f = at("top_f", [2 * NE, CAP], 27)
    flip = at("flip", [P, P], 27.5)
    w_r = at("w_r", [P, DK, NE], 28)
    logit = at("logit", [P, TT, NE], 28.5)
    aff_t = at("aff_t", [P, TT // 2, 2, NE], 30)
    rst = at("rst", [P, 2, TT], 30.5)
    cand = at("cand", [P, 2, 2, NE], 30.75)
    pick = at("pick", [P, 3, NE], 31)
    slot_i = at("slot_i", [P, NE + 2], 19.75, u32)
    slot_g = at("slot_g", [P, NE], 19.84375)
    idx = at("idx", [P, 2], 19.90625, u32)
    st2 = at("st2", [P, 8, 2], 29.375)
    idx_out = at("idx_out", [P, 1], 19.9375, u32)
    zero_i = at("zero_i", [P, 1], 19.96875, u32)
    xscr = nc.dram_tensor("xscr", [SEQ, DM], fp32, kind="Internal").ap()
    FB = 384
    NB = FF // FB
    FL = FF - (NB - 1) * FB
    wraw = at("wraw", [P, 4, DK, FL], 40)
    we_hi = at("we_hi", [P, 2, DK, FL], 96, fp32r)
    we_lo = at("we_lo", [P, 2, DK, FL], 124, fp32r)
    wdn = at("wdn", [P, 2, 4, DM], 152)
    xg = at("xg", [P, DM], 184)
    xf = at("xf", [P, DK, P], 188)
    xe_hi = at("xe_hi", [P, 2, DK, P], 192, fp32r)
    xe_lo = at("xe_lo", [P, 2, DK, P], 200, fp32r)
    sil = at("sil", [P, FL], 208)
    hid = at("hid", [P, 2, FL], 209.75)
    NS = 2
    hidT = at("hidT", [P, 2, 4 - NS, P], 213.25)
    hidT_hi = at("hidT_hi", [P, 2, NS, P], 215.25, fp32r)
    hidT_lo = at("hidT_lo", [P, 2, NS, P], 221.25, fp32r)
    wd_hi = at("wd_hi", [P, NS, DM], 20, fp32r)
    wd_lo = at("wd_lo", [P, NS, DM], 28, fp32r)
    yb = at("yb", [P, DM], 217.25)
    names4 = """wohi_ok wo_ok mshi_ok ms_ok o_ps x1_ok ssq2_ok var2_ok sd2_ok xn2_ok x2T_ps hx2_ok r_ps lg_ok
        rmx_ok rexp_ok aff_ok affT_ps affT_ok small2_in top_ok tops_ps slots_ok
        hi_ok lo_ok gu_ps sil_ok hid_ok hidT_ps hidT_ok d_ps ye_ok scat gat xx_ps xf_ok xe_ok
        wdhi_ok wdlo_ok hlo_ok""".split()
    S.update({n: sem(n) for n in names4})
    wo_in = [sem(f"wo_in{i}") for i in range(4)]
    xr_in = [sem(f"xr_in{i}") for i in range(2)]
    xst = [sem(f"xst{i}") for i in range(2)]
    wraw_in = [sem(f"wraw_in{i}") for i in range(4)]
    wdn_in = [sem(f"wdn_in{i}") for i in range(2)]

    def over_out(eng, first, second):
        first(0, 0, 0)
        first(1, 0, 1)
        second(0, 0, 0)

        def two(i):
            first(i * 2, i, 0)
            second(i * 2 - 1, i - 1, 1)
            first(i * 2 + 1, i, 1)
            second(i * 2, i, 0)

        with eng.Fori(1, TT // 2 - 1) as i:
            two(i)
        two(TT // 2 - 1)
        second(TT - 1, TT // 2 - 1, 1)

    def over_experts(eng, body):
        body(0)
        with eng.Fori(1, NE // 2) as i:
            body(i)

    def down_in(eng, i, n):
        if n < 0:
            eng.wait_ge(wdn_in[1], i * (16 * DN_TOTAL[1]))
        else:
            eng.wait_ge(wdn_in[n % 2], i * (16 * DN_TOTAL[n % 2]) + 16 * DN_AT[n])

    width = lambda b: FL if b == NB - 1 else FB
    chunks = lambda b: [(j, min(P, width(b) - j * P)) for j in range((width(b) + P - 1) // P)]
    BLOCKS = [(ee, b) for ee in (0, 1) for b in range(NB)]
    PAIR = len(BLOCKS)
    UNITS = 2 * PAIR

    DN_AT, DN_TOTAL = [], [0, 0]
    for n, (_, b) in enumerate(BLOCKS):
        DN_TOTAL[n % 2] += 2 if b == NB - 1 else 1
        DN_AT.append(DN_TOTAL[n % 2])

    block = ctx.enter_context(nc.Block())

    @block.sync
    def _(sp):
        sp.dma_start(ident[:, :], t["ident"]).then_inc(S["ident_in"], 16)
        r128 = lambda a: a.rearrange("(r p) -> r p", p=P)
        for dst, src in ((rows1[0:8], r128(t["c"][0])), (rows1[8:16], r128(t["c_ctx"])),
                         (rows1[16:24], r128(t["norm1_g"][0])), (rows1[24:32], r128(t["norm2_g"][0])),
                         (rows1[32:80], r128(t["b_mod"][0])),
                         (rows2[0:36], t["conv_w"][0].rearrange("t (r p) -> (t r) p", p=P)),
                         (rows2[36:48], r128(t["conv_b"][0])), (rows2[48:52], r128(t["hyena_bias"][0]))):
            sp.dma_start(dst, src).then_inc(S["rows_in"], 16)
        def load_wmod(n):
            j = order[n]
            if n >= 3:
                sp.wait_ge(S["mod_ps"], n - 2)
            sp.dma_start(wmod[:, n % 3, :, :],
                         t["w_mod"][0, :, j * 256:(j + 1) * 256].rearrange("(k p) c -> p k c", p=P)
                         ).then_inc(wm_in[n % 3], 16)

        for n in range(4):
            load_wmod(n)
        sp.dma_start(decay[:, :, :], t["decay"].rearrange("(t p) c -> p t c", p=P)).then_inc(S["decay_in"], 16)
        sp.dma_start(bias_b[:, :], t["hyena_bias"][0:1, :].to_broadcast([P, HYW])).then_inc(S["bias_in"], 16)
        for g, o in ((0, 2 * DM), (1, 5 * DM)):
            sp.dma_start(gate_b[0:1, g, :], t["b_mod"][0:1, o:o + DM]).then_inc(S["brow_in"], 16)
        sp.dma_start(fwd[:, :, :], t["fwd"]).then_inc(S["fwd_in"], 16)
        for n in range(4, MU):
            load_wmod(n)

        sp.wait_ge(S["mod_ps"], MU)
        for k in range(0, DK, 2):
            sp.dma_start(wqkv[:, k:k + 2, :], t["w_in"][0, k * P:(k + 2) * P, 0:QKVW].rearrange(
                "(k p) c -> p k c", p=P)).then_inc(S["wqkv_in"], 16)
        sp.dma_start(rope[:, :, :, :, :].rearrange("p t a b c -> p t (a b c)"),
                     t["rope"].rearrange("(t p) c -> p t c", p=P)).then_inc(S["small1_in"], 16)
        for i in range(4):
            sp.wait_ge(kst[i], 16 * NCLS // 4)
        sp.dma_start(head_g[:, 0, :], t["q_norm_g"][0:1, :].to_broadcast([P, HD])).then_inc(S["small1_in"], 16)
        sp.dma_start(head_g[:, 1, :], t["k_norm_g"][0:1, :].to_broadcast([P, HD])).then_inc(S["small1_in"], 16)

        def load_x(i, h, par):
            sp.wait_ge(S["xt_used"], i + 1)
            src = t["ctx"][0, bass.ts(i - TT, P), :] if is_ctx(i) else t["x"][0, bass.ts(i, P), :]
            sp.dma_start(xt[:, par, :], src).then_inc(xt_in[par], 16)

        def copy_h(i, h, par):
            if is_ctx(i):
                return
            sp.wait_ge(S["hs_ok"], i + 1)
            for dst, src in ((hT_hi, hs_hi), (hT_lo, hs_lo)):
                sp.dma_start(dst[:, :, bass.ts(i, P)].bitcast(fp32), src[:, par, :, :].bitcast(fp32)
                             ).then_inc(S["hT_in"], 16)

        over_tiles(sp, load_x, copy_h)

        def load_wh(c):
            for g in range(3):
                if isinstance(c, int) and c == 0:
                    if g == 1:
                        sp.wait_ge(S["kv_ps"], KT + 2)
                else:
                    sp.wait_ge(S["wh_ok"], c * 3 + g + 1)
                sp.dma_start(wh[g][:, :, :], t["w_in"][0, :, bass.ds(c * P + (QKVW + GROUP[g] * HYW), P)].rearrange(
                    "(k p) c -> p k c", p=P)).then_inc(wh_in[g], 16)

        over_channels(sp, load_wh, lambda c, ahead: ahead())
        sp.wait_ge(S["uT_ok"], HC + 1)
        sp.wait_ge(S["proj_ps"], 6 * HC + 6)
        sp.dma_start(fwd3[:, :, 0:FW0], t["fwd"][:, :, 0:FW0]).then_inc(S["fwd3_in"], 16)
        sp.dma_start(fwd3[:, :, FW0:FW], t["fwd"][:, :, FW0:FW]).then_inc(S["fwd3b_in"], 16)
        sp.wait_ge(S["x2_ok"], HC)
        for i in range(NCLS):
            if i == 2:
                sp.dma_start(inv_a[:, :], t["inv"][:, 0:IV + 8 * N1]).then_inc(S["inv_in"], 16)
                sp.wait_ge(S["vu_ok"], 5)
                sp.dma_start(inv_b[:, :], t["inv"][:, IV + 8 * N1:]).then_inc(S["inv_in"], 16)
            if i >= 2:
                sp.wait_ge(S["prod_ok"], i - 1)
            for side in (0, 1):
                sp.dma_start(kin[:, i % 2, side, :], kscr[side, i, :, :]).then_inc(kin_in[i % 2], 16)

        def load_wo(k):
            if k >= 4:
                sp.wait_ge(S["wo_ok"], k - 3)
            if k < NPAIR:
                for w in (0, 1):
                    r0 = (k + 4 * w) * HD
                    sp.dma_start(wo[w * HD:(w + 1) * HD, k % 4, :], t["w_out"][0, r0:r0 + HD, :]
                                 ).then_inc(wo_in[k % 4], 16)
            else:
                sp.dma_start(wo[:, k % 4, :], t["w_out"][0, k * P:(k + 1) * P, :]).then_inc(wo_in[k % 4], 16)

        sp.wait_ge(S["kT_ok"], len(KROUND))
        sp.wait_ge(S["z_ps"], HC)
        for k in range(4):
            load_wo(k)
        sp.dma_start(flip[:, :], t["flip"]).then_inc(S["small2_in"], 16)
        sp.dma_start(w_r[:, :, :], t["w_router"][0].rearrange("(k p) e -> p k e", p=P)).then_inc(S["small2_in"], 16)
        sp.wait_ge(S["pve_ok"], 2 * NPAIR)
        for k in range(4, DK):
            load_wo(k)

        def load_xr(i, h, par):
            need(sp, "x1_ok", i - 1)
            sp.dma_start(xr[:, par, :], t["x"][0, bass.ts(i, P), :]).then_inc(xr_in[par], 16)

        def store(i, h, par):
            sp.wait_ge(S["xn2_ok"], i + 1)
            sp.dma_start(out[0, bass.ts(i, P), :], x1[:, par, :]).then_inc(xst[par], 16)
            sp.dma_start(xscr[bass.ts(i, P), :], xn2[:, par, :]).then_inc(xst[par], 16)

        over_out(sp, load_xr, store)
        for i in (0, 1):
            sp.wait_ge(xst[i], 16 * TT + 32)
        sp.wait_ge(S["o_ps"], TT)
        sp.wait_ge(S["r_ps"], TT)

        def load_down(i, n):
            ee, b = (-1, NB - 1) if n < 0 else BLOCKS[n]
            w, c0 = width(b), b * FB
            need(sp, "d_ps", i * PAIR + (n - 1))
            full = w // P
            wd = t["w_down"][0, bass.ds(i * 2 + ee, 1), :, :].squeeze(0)
            sp.dma_start(wdn[:, n % 2, 0:full, :], wd[c0:c0 + full * P, :].rearrange("(j p) c -> p j c", p=P)
                         ).then_inc(wdn_in[n % 2], 16)
            if w % P:
                sp.dma_start(wdn[0:w % P, n % 2, full, :], wd[c0 + full * P:c0 + w, :]).then_inc(wdn_in[n % 2], 16)

        def load_experts(i):
            for n, (ee, b) in enumerate(BLOCKS):
                w, c0 = width(b), b * FB
                for m, name in ((0, "w_gate"), (1, "w_up")):
                    u = 2 * n + m
                    need(sp, "lo_ok", i * UNITS + (u - 3))
                    sp.dma_start(wraw[:, u % 4, :, 0:w],
                                 t[name][0, bass.ds(i * 2 + ee, 1), :, c0:c0 + w].squeeze(0).rearrange(
                                     "(k p) c -> p k c", p=P)).then_inc(wraw_in[u % 4], 16)
                if not (isinstance(i, int) and n == 0):
                    load_down(i, n - 1)

        over_experts(sp, load_experts)
        load_down(NE // 2, -1)
        sp.wait_ge(S["scat"], 16 * NE)

    @block.gpsimd
    def _(pool):
        for i in range(KT):
            if i >= 2:
                pool.wait_ge(S["xs_used"], i - 1)
            src = t["x"][0, i * P:(i + 1) * P, :] if i < TT else t["ctx"][0, (i - TT) * P:(i - TT + 1) * P, :]
            pool.dma_start(xstat[:, i % 2, :], src).then_inc(xs_in[i % 2], 16)
        for n in range(2 * NCLS):
            pool.wait_ge(S["kmul"], n + 1)
            pool.wait_ge(S["kadd"], min(n, NCLS) + 1)
            pool.dma_start(kscr[n // NCLS, n % NCLS, :, :], kslot(n)).then_inc(kst[n % 4], 16)
        for i in range(4):
            pool.wait_ge(kst[i], 16 * NCLS // 2)

        pool.wait_ge(S["small1_in"], 48)
        pool.tensor_scalar(head_g[:, 0, :], head_g[:, 0, :], HD ** -0.5, None, ALU.mult)
        pool.drain()

        def turn(i, h, par):
            pool.wait_ge(S["qn_ok"], i + 3)
            if is_ctx(i):
                pool.tensor_tensor(qk_all[:, bass.ds(i, 1), NQ:NH, :].squeeze(1), qn[:, NQ:NH, :],
                                   head_g[:, 1:2, :].to_broadcast([P, NKV, HD]), ALU.mult).then_inc(S["qk_ok"], 1)
                return
            for w, a, b in ((0, 0, NQ), (1, NQ, NH)):
                pool.tensor_tensor(qn[:, a:b, :], qn[:, a:b, :], head_g[:, w:w + 1, :].to_broadcast([P, b - a, HD]),
                                   ALU.mult)
            pool.drain()
            xin = qn[:, :, :].rearrange("p n (a b c) -> p n a b c", a=2, b=2)
            yout = qk_all[:, bass.ds(i, 1), :, :].squeeze(1).rearrange("p n (a b c) -> p n a b c", a=2, b=2)
            tmp = [rtmp[:, w, :].rearrange("p (n a c) -> p n a c", n=NH, a=2) for w in (0, 1)]
            tab = [rope[:, bass.ds(i, 1), w, :, :].to_broadcast([P, NH, 2, HD // 4]) for w in (0, 1)]
            x1, x2 = xin[:, :, :, 0, :], xin[:, :, :, 1, :]
            for half, (u0, u1, op) in enumerate(((0, 1, ALU.subtract), (1, 0, ALU.add))):
                pool.tensor_tensor(tmp[0], x1, tab[u0], ALU.mult)
                pool.tensor_tensor(tmp[1], x2, tab[u1], ALU.mult)
                pool.drain()
                last = pool.tensor_tensor(yout[:, :, :, half, :], tmp[0], tmp[1], op)
                if half == 0:
                    pool.drain()
            last.then_inc(S["qk_ok"], 1)

        over_tiles(pool, lambda i, h, par: None, turn)

        for i in range(NCLS):
            pool.wait_ge(S["prod_ok"], i + 1)
            pr = prod[:, i % 2, :, :]
            pool.tensor_tensor(yspec[:, i, 0, :], pr[:, 0, :], pr[:, 1, :], ALU.subtract)
            last = pool.tensor_tensor(yspec[:, i, 1, :], pr[:, 2, :], pr[:, 3, :], ALU.add)
            if i == 0:
                pool.drain()
                for w in (0, 1):
                    last = pool.tensor_copy(yspec[0:1, i, w, :], prod[0:1, 0, w, :])
            last.then_inc(S["y_ok"], 1)

        with pool.Fori(0, NPAIR * STEPS // 4) as g:
            for m in range(4):
                pool.wait_ge(S["rs_ok"], g * 4 + m + 1)
                pool.tensor_tensor(prob[:, m, :], prob[:, m, :], prcp[:, m:m + 1].to_broadcast([P, KT * P]),
                                   ALU.mult).then_inc(S["pn_ok"], 1)

        off = lambda a: bass.IndirectOffsetOnAxis(ap=a, axis=0)
        pool.wait_ge(S["slots_ok"], 1)
        for i in (0, 1):
            pool.wait_ge(xst[i], 16 * TT + 32)

        pool.memset(zero_i[:, :], 0)
        pool.drain()

        def gather(slot):
            pool.indirect_dma_start(xg[:, :], None, xscr, off(idx[:, slot:slot + 1])).then_inc(S["gat"], 16)

        pool.tensor_copy(idx[:, :], slot_i[:, 0:2])
        pool.drain()
        gather(0)
        pool.wait_ge(S["xx_ps"], 2)
        pool.tensor_copy(idx_out[:, :], slot_i[:, 0:1])
        pool.drain()
        gather(1)

        def experts(i):
            for ee in (0, 1):
                e = i * 2 + ee
                pool.wait_ge(S["ye_ok"], e + 1)
                pool.tensor_tensor(idx_out[:, :], idx[:, ee:ee + 1], zero_i[:, :], ALU.add)
                pool.drain()
                pool.tensor_copy(idx[:, ee:ee + 1], slot_i[:, bass.ds(e + 2, 1)])
                pool.drain()
                pool.indirect_dma_start(out[0], off(idx_out[:, :]), yb[:, :], None, compute_op=ALU.add
                                        ).then_inc(S["scat"], 16)
                gather(ee)

        over_experts(pool, experts)
        pool.wait_ge(S["gat"], 16 * (NE + 2))

    @block.tensor
    def _(pe):
        pe.wait_ge(S["ident_in"], 16)
        pe.wait_ge(S["rows_in"], 8 * 16)
        pe.transpose(bank[7][:, 0:80], rows1[:, :], ident[0:80, 0:80])
        pe.transpose(bank[7][:, 80:132], rows2[:, :], ident[0:52, 0:52]).then_inc(S["cols_ps"], 1)
        pe.wait_ge(S["filt_in"], 7 * 16)
        for h in (0, 1):
            last = pe.matmul(bank[h][0:ORD, :], fw1[:, :], feat[:, h * 512:(h + 1) * 512], start=True, stop=True)
        last.then_inc(S["l1_ps"], 1)

        def unit(n):
            mod_unit(pe, n, order[n])
            m = n - 1
            if 0 <= m < len(rowu):
                pe.wait_ge(S["mrow_ok"], m + 1)
                for h in (0, 1):
                    last = pe.transpose(bank[7][:, 4 * m + 2 * h:4 * m + 2 * h + 2],
                                        mod_row[:, m % 2, h * P:(h + 1) * P], ident[0:2, 0:2])
                if m == len(rowu) - 1:
                    last.then_inc(S["mtr_ps"], 1)

        pe.wait_ge(S["silu_ok"], 1)
        unit(0)
        unit(1)
        pe.wait_ge(S["sin_ok"], 1)
        for h in (0, 1):
            last = pe.matmul(bank[2 + h][0:ORD, :], fw2[:, :], fsin[:, 0, h, :], start=True, stop=True)
        last.then_inc(S["l2_ps"], 1)
        unit(2)
        unit(3)
        pe.wait_ge(S["sin_ok"], 2)
        for i in range(2 * TT):
            tt, side = i // 2, i % 2
            if i >= 4:
                pe.wait_ge(S["h_ok"], i - 3)
            pe.matmul(bank[i % 4][:, :], fsin[:, 1, tt // 4, (tt % 4) * P:(tt % 4 + 1) * P],
                      fw3[:, side * HYW:(side + 1) * HYW], start=True, stop=True).then_inc(S["l3_ps"], 1)
        unit(4)
        for n in range(5, STAT0):
            unit(n)
        pe.wait_ge(S["habs_sum"], 1)
        pe.wait_ge(S["ones_ok"], 1)
        pe.matmul(bank[6][:, :], ones[:, :], habs[:, 0, 0:HYW], start=True, stop=True).then_inc(S["norm_ps"], 1)
        for n in range(STAT0, MU):
            if order[n] in gatu:
                pe.wait_ge(S["silub_ok"], 1)
                pe.wait_ge(S["brow_in"], 2 * 16)
            unit(n)

        def tile_transposes(i):
            pe.wait_ge(S["xn_ok"], i + 1)
            pe.wait_ge(S["full_ok"], i + 1)
            for k in range(DK):
                last = pe.transpose(bank[6 + k // 4][:, (k % 4) * P:(k % 4 + 1) * P], xn[:, k * P:(k + 1) * P],
                                    ident[:, :])
            last.then_inc(S["xT_ps"], 1)

        pe.wait_ge(S["fwd_in"], 16)
        pe.wait_ge(S["h_ok"], 2 * TT)
        for i in range(2 * NCLS):
            side, tile = i // NCLS, i % NCLS
            pe.wait_ge(S["v_ok"], 5 * side + STAGE[tile])
            if i >= 4:
                pe.wait_ge(S["kmul"], i - 3)
            transform(pe, bank[i % 4], side, tile, (vsum, vdif)[side], vsum, fwd).then_inc(S["kps"], 1)
            if i == 2 * NCLS - 3:
                tile_transposes(0)


        def x_transposes(i, h, par):
            if not (isinstance(i, int) and i == 0):
                tile_transposes(i)

        def qkv(i, h, par):
            pe.wait_ge(S["hs_ok"], i + 1)
            pe.wait_ge(S["qn_ok"], i + 1)
            parts = [(bank[2 + par], 0, QW), (bank[4 + par], QW, QKVW)]
            for ps, a, b in parts[1 if is_ctx(i) else 0:]:
                for k in range(DK):
                    last = split3(pe, ps[:, 0:b - a], hs_hi[:, par, k, :], hs_lo[:, par, k, :],
                                  wqkv_hi[:, k, a:b], wqkv_lo[:, k, a:b], k == 0, k == DK - 1)
            last.then_inc(S["kv_ps"], 1)

        pe.wait_ge(S["wqkvlo_ok"], DK)
        over_tiles(pe, x_transposes, qkv)

        def hyena_products(c, ahead):
            for g in range(3):
                pe.wait_ge(S["wh_ok"], c * 3 + g + 4)
                if isinstance(c, int) and c == 0 and g == 1:
                    pe.wait_ge(S["qn_ok"], KT + 2)
                for h in (0, 1):
                    n = 2 * g + h
                    pe.wait_ge(S["evac_ok"], c * 6 + n + 1)
                    for k in range(DK):
                        last = split3(pe, bank[n][:, :], wh_hi[:, g, k, :], wh_lo[:, g, k, :],
                                      hT_hi[:, k, h * 512:(h + 1) * 512], hT_lo[:, k, h * 512:(h + 1) * 512],
                                      k == 0, k == DK - 1)
                    last.then_inc(S["proj_ps"], 1)
            pe.wait_ge(S["u_ok"], c + 1)
            pe.wait_ge(S["uT_ok"], c + 1)
            for tt in range(TT):
                last = pe.transpose(bank[6 + tt // 4][:, (tt % 4) * P:(tt % 4 + 1) * P],
                                    gated[:, tt * P:(tt + 1) * P], ident[:, :])
            last.then_inc(S["uT_ps"], 1)

        pe.wait_ge(S["hT_in"], 64 + 32 * TT)
        pe.wait_ge(S["full_ok"], KT + 1)
        over_channels(pe, lambda c: None, hyena_products)
        pe.wait_ge(S["uT_ok"], HC + 1)
        pe.wait_ge(S["evac_ok"], 6 * HC + 6)
        pe.wait_ge(S["fwd3_in"], 16)
        for i in range(NCLS):
            if i == 2:
                pe.wait_ge(S["fwd3b_in"], 16)
            if i >= 4:
                pe.wait_ge(S["prod_ok"], i - 3)
            pe.wait_ge(S["vu_ok"], STAGE[i])
            for side in (0, 1):
                transform(pe, bank[2 * (i % 4) + side], side, i, vu, vu, fwd3).then_inc(S["us_ps"], 1)
        pe.wait_ge(S["prod_ok"], 6)
        for n, (w, kv, a) in enumerate(KROUND):
            pe.wait_ge(S[("kshi_ok", "kslo_ok")[w]], 1)
            if n >= 4:
                pe.wait_ge(S["kT_ok"], n - 3)
            for j in range(a, min(a + 4, KT)):
                last = pe.transpose(bank[n % 4][:, (j - a) * P:(j - a + 1) * P],
                                    (ks_hi, ks_lo)[w][:, j, kv, :, :].rearrange("p a b -> p (a b)").bitcast(fp32),
                                    ident[:, :])
            last.then_inc(S["kT_ps"], 1)
        pe.wait_ge(S["kT_ok"], len(KROUND))
        pe.wait_ge(S["prod_ok"], NCLS)
        pe.wait_ge(S["inv_in"], 2 * 16)
        for c in range(HC):
            ch = slice(c * P, (c + 1) * P)
            if c >= 2:
                pe.wait_ge(S["z_ok"], c - 1)
            zb = [bank[4 * (c % 2) + z] for z in range(4)]
            pe.wait_ge(S["y_ok"], NCLS)
            for tile in (0, 1):
                for w in (0, 1):
                    col = (2 * tile + w) * N1
                    pe.matmul(zb[0][:, tile * N1:(tile + 1) * N1], yspec[:, tile, w, ch], inv_a[:, col:col + N1],
                              start=(w == 0), stop=(w == 1))
            for k2 in (1, 2, 3):
                for m in range(4):
                    tile, w = 2 * k2 + m // 2, m % 2
                    inv, col = (inv_a, IV + m * 2 * N1) if k2 == 1 else (inv_b, ((k2 - 2) * 4 + m) * 2 * N1)
                    last = pe.matmul(zb[k2][:, :], yspec[:, tile, w, ch], inv[:, col:col + 512],
                                     start=(m == 0), stop=(m == 3))
            last.then_inc(S["z_ps"], 1)

        pe.wait_ge(S["z_ok"], HC)

        def q_round(r, hh, half, ps):
            pe.wait_ge(S["qslo_ok"], r * 2 + hh + 1)
            for j in range(4):
                last = pe.transpose(ps[:, j * P:(j + 1) * P],
                                    qs[:, hh, 4 * half + j, :, :].rearrange("p a b -> p (a b)").bitcast(fp32),
                                    ident[:, :])
            return last

        for hh in (0, 1):
            q_round(0, hh, 0, bank[6 + hh]).then_inc(S["kT_ps"], 1)
        pe.wait_ge(S["kT_ok"], len(KROUND) + 2)

        def scores(s, j, a, z):
            half, hh, qt = s // 8, s // 4 % 2, s % 4
            ps = bank[3 * (s % 2) + j][:, 0:(z - a) * P]
            q = qT[:, hh, (4 * half + qt) * P:(4 * half + qt + 1) * P]
            pe.matmul(ps, q, kT_hi[:, hh, a * P:z * P], start=True, stop=False)
            return pe.matmul(ps, q, kT_lo[:, hh, a * P:z * P], start=False, stop=True)

        def values(r, s):
            for kt in range(KT):
                for hh in (0, 1):
                    last = pe.matmul(bank[V_BANK][hh * HD:(hh + 1) * HD, :], v_all[:, kt, hh * HD:(hh + 1) * HD],
                                     probT[:, hh, kt, :], start=(kt == 0), stop=(kt == KT - 1))
            last.then_inc(S["pv_ps"], 1)

        def attend(r, kind):
            for s, rounds in enumerate(ROUNDS[kind]):
                def transposes(n):
                    if n >= len(rounds):
                        return
                    k, what = rounds[n][:2]
                    copied(pe, r, kind, k - 2)
                    if what == "p":
                        b, (a, z) = (s - LAG) % STEPS, TROUND[n]
                        if n == 0:
                            pe.wait_ge(S["pn_ok"], r * STEPS + (s - LAG + 1))
                        for kt in range(a, z):
                            last = pe.transpose(bank[6 + k % 2][:, (kt - a) * P:(kt - a + 1) * P],
                                                prob[:, b % 4, kt * P:(kt + 1) * P], ident[:, :])
                    else:
                        hh, half = rounds[n][2:]
                        last = q_round(r + (1 - half), hh, half, bank[6 + k % 2])
                    last.then_inc(S["t_ps"], 1)

                transposes(0)
                transposes(1)
                if kind != "tail":
                    pe.wait_ge(S["p_ok"], r * STEPS + s + 1)
                    if s == 0 and kind != "first":
                        copied(pe, r, kind, ROUNDS["mid"][14][-1][0] - RB)
                    if s == 8:
                        copied(pe, r, kind, ROUNDS[kind][5][-1][0])
                    if s == V_SLOT[1] + 1 or (s == V_SLOT[0] + 1 and kind != "first"):
                        pe.wait_ge(S["pve_ok"], r * 2 + (s > 8))
                    scores(s, 0, *TROUND[0])
                transposes(2)
                if kind != "tail":
                    scores(s, 1, *TROUND[1])
                    scores(s, 2, *TROUND[2]).then_inc(S["s_ps"], 1)
                transposes(3)
                if s == V_SLOT[1] or (s == V_SLOT[0] and kind != "first"):
                    copied(pe, r, kind, thirds_done(kind, s) - 1)
                    copied(pe, r, kind, thirds_done(kind, s))
                    if kind != "tail":
                        pe.wait_ge(S["p_ok"], r * STEPS + (s + 2))
                    values(r, s)

        over_pairs(pe, attend)

        pe.wait_ge(S["pve_ok"], 2 * NPAIR)
        copied(pe, NPAIR, "tail", thirds_done("tail", LAG - 1) - 1)
        pe.wait_ge(S["p_ok"], NPAIR * STEPS + 2)

        def project(i, h, par):
            pe.wait_ge(S["ms_ok"], i + 1)
            need(pe, "x1_ok", i - 1)
            for half in (0, 1):
                for k in range(DK):
                    if isinstance(i, int) and i == 0 and half == 0:
                        pe.wait_ge(S["wo_ok"], k + 1)
                    last = split3(pe, bank[2 * par + half][:, :], ms_hi[:, par, k, :], ms_lo[:, par, k, :],
                                  wo_hi[:, k, half * 512:(half + 1) * 512], wo_lo[:, k, half * 512:(half + 1) * 512],
                                  k == 0, k == DK - 1)
            last.then_inc(S["o_ps"], 1)

        def route(i, h, par):
            pe.wait_ge(S["xn2_ok"], i + 1)
            need(pe, "hx2_ok", i)
            for k in range(DK):
                last = pe.transpose(bank[4 + k // 4][:, (k % 4) * P:(k % 4 + 1) * P], xn2[:, par, k * P:(k + 1) * P],
                                    ident[:, :])
            last.then_inc(S["x2T_ps"], 1)
            if not (isinstance(i, int) and i == 0):
                logits(i - 1, 1 - par)

        def logits(i, par):
            need(pe, "lg_ok", i)
            for k in range(DK):
                last = pe.matmul(bank[6][:, 0:NE], hs2[:, par, k, :], w_r[:, k, :], start=(k == 0), stop=(k == DK - 1))
            last.then_inc(S["r_ps"], 1)

        pe.wait_ge(S["small2_in"], 32)
        over_out(pe, project, route)
        pe.wait_ge(S["hx2_ok"], TT)
        logits(TT - 1, 1)
        pe.wait_ge(S["aff_ok"], 1)
        for i in range(TT // 2):
            last = pe.transpose(bank[4][0:2 * NE, i * P:(i + 1) * P], aff_t[:, i, :, :].rearrange("p a b -> p (a b)"),
                                ident[:, :])
        last.then_inc(S["affT_ps"], 1)
        pe.wait_ge(S["top_ok"], 1)
        pe.transpose(bank[6][:, 0:2 * NE], top_v[:, :], ident[0:2 * NE, 0:2 * NE])
        pe.transpose(bank[6][:, 2 * NE:4 * NE], top_f[:, :], ident[0:2 * NE, 0:2 * NE]).then_inc(S["tops_ps"], 1)
        pe.wait_ge(S["top_ok"], 2)
        pe.matmul(bank[7][:, 0:4 * NE], flip[:, :], cand[:, :, :, :].rearrange("p a b c -> p (a b c)"),
                  start=True, stop=True).then_inc(S["tops_ps"], 1)
        def token_transposes(e, q, ps):
            pe.wait_ge(S["gat"], e * 16 + 16)
            for k in range(4):
                last = pe.transpose(ps[:, k * P:(k + 1) * P], xg[:, (4 * q + k) * P:(4 * q + k + 1) * P], ident[:, :])
            last.then_inc(S["xx_ps"], 1)

        def unit(i, n, ee, b, m):
            u, w = 2 * n + m, width(b)
            pe.wait_ge(S["lo_ok"], i * UNITS + (u + 1))
            if m == 0:
                need(pe, "hid_ok", i * PAIR + (n - 1))
                if b == 0:
                    pe.wait_ge(S["xe_ok"], i * 2 + (ee + 1))
            for k in range(DK):
                last = split3(pe, bank[2 * (n % 2) + m][:, 0:w], xe_hi[:, ee, k, :], xe_lo[:, ee, k, :],
                              we_hi[:, m, k, 0:w], we_lo[:, m, k, 0:w], k == 0, k == DK - 1)
            last.then_inc(S["gu_ps"], 1)

        def hidden_transposes(i, n, b):
            pe.wait_ge(S["hid_ok"], i * PAIR + (n + 1))
            need(pe, "hlo_ok", i * PAIR + (n - 1))
            if b in (3, 4):
                e = i * 2 + (1 if n >= NB else 0)
                pe.wait_ge(S["xf_ok"], e * 2 + (b))
            for j, c in chunks(b):
                last = pe.transpose(bank[4 + n % 2][0:c, j * P:(j + 1) * P], hid[:, n % 2, j * P:j * P + c], ident[:, :])
            last.then_inc(S["hidT_ps"], 1)

        def down(i, n, b):
            pe.wait_ge(S["hlo_ok"], i * PAIR + (n + 1))
            pe.wait_ge(S["wdlo_ok"], i * PAIR + (n + 1))
            down_in(pe, i, n)
            if b == 0:
                need(pe, "ye_ok", i * 2 + (1 if n >= NB else 0))
            for j, c in chunks(b):
                for half in (0, 1):
                    first, final = b == 0 and j == 0, b == NB - 1 and j == len(chunks(b)) - 1
                    cs = slice(half * 512, (half + 1) * 512)
                    if j < NS:
                        last = split3(pe, bank[6 + half][:, :], hidT_hi[:, n % 2, j, :], hidT_lo[:, n % 2, j, :],
                                      wd_hi[:, j, cs], wd_lo[:, j, cs], first, final)
                    else:
                        last = pe.matmul(bank[6 + half][:, :], hidT[0:c, n % 2, j - NS, :], wdn[0:c, n % 2, j, cs],
                                         start=first, stop=final)
            last.then_inc(S["d_ps"], 1)

        def experts(i):
            for n, (ee, b) in enumerate(BLOCKS):
                before = not (isinstance(i, int) and i == 0 and n == 0)
                pb = BLOCKS[n - 1][1]
                unit(i, n, ee, b, 0)
                if before:
                    hidden_transposes(i, n - 1, pb)
                unit(i, n, ee, b, 1)
                if before:
                    down(i, n - 1, pb)
                if b in (2, 3):
                    token_transposes(i * 2 + (ee + 1), b - 2, bank[4 + (n - 1) % 2])

        pe.wait_ge(S["affT_ok"], 1)
        for q in (0, 1):
            token_transposes(0, q, bank[4 + q])
        pe.wait_ge(S["xf_ok"], 2)
        pe.wait_ge(S["slots_ok"], 1)
        over_experts(pe, experts)
        hidden_transposes(NE // 2, -1, NB - 1)
        down(NE // 2, -1, NB - 1)

    @block.scalar
    def _(act):
        one = lambda a: a.rearrange("(p o) -> p o", o=1)
        with nc.allow_non_contiguous_dma(reason="three columns of 64"):
            for dst, src in ((feat[:, :], t["feat"]), (fw1[:, :], t["filt_w1"][0]), (fw2[:, :], t["filt_w2"][0]),
                             (fcol[:, 0:1], one(t["filt_b1"][0])), (fcol[:, 1:2], one(t["filt_b2"][0])),
                             (fcol[:, 2:3], one(t["filt_freq"][0])), (fw3[:, :], t["filt_w3"][0])):
                act.dma_start(dst, src).then_inc(S["filt_in"], 16)
        def stats(i):
            act.wait_ge(xs_in[i % 2], 16 * (i // 2 + 1))
            for h in (0, 1):
                last = act.activation(bank[6][:, :], xstat[:, i % 2, h * 512:(h + 1) * 512], ACT.Square,
                                      accum_out=stat[:, h, i:i + 1])
                act.drain()
            act.sem_inc(S["xs_used"], 1)

        act.wait_ge(S["cols_ok"], 1)
        for v, c in ((0, C_C), (1, C_CC)):
            last = act.activation(silu_c[:, :, v], cols[:, c:c + DK], ACT.Silu)
        last.then_inc(S["silu_ok"], 1)

        def rows_out(n):
            act.wait_ge(S["mod_ps"], n + 1)
            ps = bank[4 + n % 2]
            if order[n] in gatu:
                g, o = gatu.index(order[n]) // 4, (gatu.index(order[n]) % 4) * 256
                last = act.activation(gate_b[:, g, o:o + 256], ps[:, 0:256], ACT.Copy)
            else:
                last = act.activation(mod_row[:, n % 2, :], ps[0:2, 0:256], ACT.Copy)
            last.then_inc(S["mrow_ok"], 1)

        for layer in (0, 1):
            act.wait_ge(S["sin_in"], layer + 1)
            act.activation(fsin[:, layer, :, :], farg[:, :, :], ACT.Sin).then_inc(S["sin_ok"], 1)
            rows_out(2 * layer)
            rows_out(2 * layer + 1)
        act.wait_ge(S["h_ok"], 2 * TT + 1)
        act.activation(habs[:, 0, :], hfwd[:, :, :].rearrange("p a b -> p (a b)"), ACT.Abs)
        act.activation(habs[:, 1, :], hbwd[:, :, :].rearrange("p a b -> p (a b)"), ACT.Abs).then_inc(S["habs_ok"], 1)
        for n in range(4, STAT0):
            rows_out(n)
        act.wait_ge(S["invn_ok"], 1)
        for i in range(KT):
            stats(i)
            rows_out(STAT0 + i)
        act.sem_inc(S["ssq_ok"], 1)
        act.wait_ge(S["var_ok"], 1)
        act.activation(stat[:, 2, :], stat[:, 1, :], ACT.Sqrt).then_inc(S["sqrt_ok"], 1)
        for n in range(STAT0 + KT, MU):
            rows_out(n)

        act.wait_ge(S["v_ok"], 10)
        for k in range(DK):
            if k % 2 == 0:
                act.wait_ge(S["wqkv_in"], 16 * DK // 2)
            act.activation(wqkv_hi[:, k, :], wqkv[:, k, :], ACT.Copy).then_inc(S["wqkvhi_ok"], 1)

        def modulate1(i, h, par):
            w = 1 if is_ctx(i) else 0
            act.wait_ge(S["xT_ps"], i + 1)
            need(act, "hs_ok", i)
            for k in range(DK):
                last = act.activation(hfull[:, k, :], bank[6 + k // 4][:, (k % 4) * P:(k % 4 + 1) * P], ACT.Identity,
                                      bias=mod_t[:, k, w:w + 1], scale=scale1[:, k, w:w + 1])
            last.then_inc(S["full_ok"], 1)

        def high_wh(c, g):
            act.activation(wh_hi[:, g, :, :], wh[g][:, :, :], ACT.Copy).then_inc(S["whhi_ok"], 1)

        def squares(i, h, par):
            if isinstance(i, int) and i == KT - 1:
                act.wait_ge(S["xn_ok"], KT)
                act.wait_ge(wh_in[0], 16)
                high_wh(0, 0)
            act.wait_ge(S["kv_ps"], i + 3)
            need(act, "qvar_ok", i)
            flat = qsq[:, :, :].rearrange("p a b -> p (a b)")
            if not is_ctx(i):
                act.activation(flat[:, 0:QW], bank[2 + par][:, :], ACT.Square)
            act.activation(flat[:, QW:QKW], bank[4 + par][:, 0:QKW - QW], ACT.Square)
            act.activation(v_all[:, bass.ds(i, 1), :], bank[4 + par][:, QKW - QW:QKVW - QW], ACT.Copy
                           ).then_inc(S["sq_ok"], 1)
            act.wait_ge(S["qvar_ok"], i + 1)
            g = slice(NQ, NH) if is_ctx(i) else slice(0, NH)
            act.activation(qst[:, 1, g], qst[:, 0, g], ACT.Sqrt).then_inc(S["qsd_ok"], 1)

        act.wait_ge(S["wqkvlo_ok"], DK)
        over_tiles(act, modulate1, squares)

        act.wait_ge(S["kv_ps"], KT + 2)
        act.wait_ge(S["qk_ok"], KT)
        act.wait_ge(S["hT_in"], 64 + 32 * TT)

        def split_wh(c):
            for g in range(3):
                if isinstance(c, int) and c == 0 and g == 0:
                    continue
                act.wait_ge(wh_in[g], c * 16 + 16)
                act.wait_ge(S["proj_ps"], c * 6 + 2 * g + 2)
                high_wh(c, g)

        def evacuate(c, ahead):
            for g in range(3):
                act.wait_ge(S["conv_ok"], c * 3 + g + 1)
                for h in (0, 1):
                    n = 2 * g + h
                    act.wait_ge(S["proj_ps"], c * 6 + n + 7)
                    act.activation(pad[:, g, 1 + h * 512:1 + (h + 1) * 512], bank[n][:, :], ACT.Copy
                                   ).then_inc(S["evac_ok"], 1)
                if g == 1:
                    ahead()
            act.wait_ge(S["uT_ps"], c + 1)
            for b in (0, 1):
                last = act.activation(uT[:, 4 * b:4 * b + 4, bass.ts(c, P)],
                                      bank[6 + b][:, :].rearrange("p (a b) -> p a b", b=P), ACT.Copy)
            last.then_inc(S["uT_ok"], 1)

        over_channels(act, split_wh, evacuate)
        act.wait_ge(S["us_ps"], 2 * NCLS)
        for w in (0, 1):
            last = act.activation(ks_hi[:, :, :, w, :], qk_all[:, :, NQ:NH, :], ACT.Copy)
        last.then_inc(S["kshi_ok"], 1)
        for n, (w, kv, a) in enumerate(KROUND):
            act.wait_ge(S["kT_ps"], n + 1)
            z = min(a + 4, KT)
            act.activation((kT_hi, kT_lo)[w][:, kv, a * P:z * P], bank[n % 4][:, 0:(z - a) * P], ACT.Copy
                           ).then_inc(S["kT_ok"], 1)
        for c in range(HC):
            act.wait_ge(S["z_ps"], c + 1)
            if c >= 2:
                act.wait_ge(S["mixhy_ok"], c - 1)
            for z in range(4):
                last = act.activation(zs[:, c % 2, z, :], bank[4 * (c % 2) + z][:, :], ACT.Copy)
            last.then_inc(S["z_ok"], 1)


        def high_q(r):
            for hh in (0, 1):
                act.activation(qs[:, hh, :, 0, :], qk_all[:, 0:TT, bass.ds(r + 4 * hh, 1), :].squeeze(2), ACT.Copy
                               ).then_inc(S["qshi_ok"], 1)

        def queries_out(hh, half, ps):
            return act.activation(qT[:, hh, half * 512:(half + 1) * 512], ps[:, :], ACT.Copy)

        high_q(0)
        for hh in (0, 1):
            act.wait_ge(S["kT_ps"], len(KROUND) + hh + 1)
            queries_out(hh, 0, bank[6 + hh]).then_inc(S["kT_ok"], 1)
        act.wait_ge(S["at_free"], 1)

        def soften(r, kind):
            for s, rounds in enumerate(ROUNDS[kind]):
                for n in range(max(3, len(rounds))):
                    if n == 2 and not (kind == "first" and s == 0) and not (kind == "tail" and s > 0):
                        e = (s - 1) % STEPS
                        act.wait_ge(S["mx_ok"], r * STEPS + s)
                        if not (kind == "first" and s < 5):
                            act.wait_ge(S["t_ps"], r * RB + (thirds_done(kind, s - 5 + LAG) + 1))
                        act.activation(prob[:, e % 4, :], psum[:, SET * (e % 2):SET * (e % 2) + KT * P], ACT.Exp,
                                       bias=nmax[:, e % 4:e % 4 + 1], accum_out=psums[:, e % 4:e % 4 + 1]
                                       ).then_inc(S["p_ok"], 1)
                    if n >= len(rounds) or rounds[n][1:] == ("p", 2):
                        continue
                    k, what = rounds[n][:2]
                    act.wait_ge(S["t_ps"], r * RB + (k + 1))
                    if what == "p":
                        b, (a, z) = (s - LAG) % STEPS, TROUND[n]
                        if b % 8 == 0 and n == 0 and not (kind == "first" and s == LAG):
                            act.wait_ge(S["pv_ps"], r * 2 + b // 8)
                        last = act.activation(probT[:, b // 4 % 2, a:z, (b % 4) * P:(b % 4 + 1) * P],
                                              bank[6 + k % 2][:, 0:(z - a) * P].rearrange("p (a b) -> p a b", b=P),
                                              ACT.Copy)
                    else:
                        last = queries_out(*rounds[n][2:], bank[6 + k % 2])
                    last.then_inc(S["te_ok"], 1)
                if s == 8 and kind != "last":
                    high_q(r + 1)

        over_pairs(act, soften)

        act.wait_ge(S["pve_ok"], 2 * NPAIR)

        def high_mix(i, par):
            need(act, "o_ps", i - 1)
            act.activation(ms_hi[:, par, 0:4, :], mix_at[:, :, bass.ts(i, P)], ACT.Copy)
            act.activation(ms_hi[:, par, 4:8, :], mix_hy[:, :, bass.ts(i, P)], ACT.Copy).then_inc(S["mshi_ok"], 1)

        def ahead_mix(i, h, par):
            if not (isinstance(i, int) and i == TT - 1):
                high_mix(i + 1, 1 - par)

        def second_norm(i, h, par):
            act.wait_ge(S["x1_ok"], i + 1)
            act.activation(junk[:, :], x1[:, par, :], ACT.Square, accum_out=st2[:, 0, par:par + 1]
                           ).then_inc(S["ssq2_ok"], 1)
            act.wait_ge(S["var2_ok"], i + 1)
            act.activation(st2[:, 2, par:par + 1], st2[:, 1, par:par + 1], ACT.Sqrt).then_inc(S["sd2_ok"], 1)
            act.wait_ge(S["x2T_ps"], i + 1)
            for k in range(DK):
                last = act.activation(hs2[:, par, k, :], bank[4 + k // 4][:, (k % 4) * P:(k % 4 + 1) * P],
                                      ACT.Identity, bias=mod_t[:, 3 * DK + k, 0:1], scale=scale2[:, k:k + 1])
            last.then_inc(S["hx2_ok"], 1)
            if not (isinstance(i, int) and i == 0):
                logits_out(i - 1)

        def logits_out(i):
            act.wait_ge(S["r_ps"], i + 1)
            act.activation(logit[:, bass.ds(i, 1), :].squeeze(1), bank[6][:, 0:NE], ACT.Copy).then_inc(S["lg_ok"], 1)

        high_mix(0, 0)
        for k in range(DK):
            act.wait_ge(wo_in[k % 4], 32 if k < NPAIR else 48)
            act.activation(wo_hi[:, k, :], wo[:, k % 4, :], ACT.Copy).then_inc(S["wohi_ok"], 1)
        over_out(act, ahead_mix, second_norm)
        logits_out(TT - 1)
        act.wait_ge(S["rmx_ok"], 1)
        act.activation(logit[:, :, :], logit[:, :, :], ACT.Exp).then_inc(S["rexp_ok"], 1)
        act.wait_ge(S["affT_ps"], 1)
        act.activation(aff[:, 0, :], bank[4][0:2 * NE, :], ACT.Copy).then_inc(S["affT_ok"], 1)
        def token_out(e, q, ps):
            act.wait_ge(S["xx_ps"], e * 2 + (q + 1))
            need(act, "xe_ok", e)
            for k in range(4):
                kk = 4 * q + k
                last = act.activation(xf[:, kk, :], ps[:, k * P:(k + 1) * P], ACT.Identity,
                                      bias=mod_t[:, 3 * DK + kk, 0:1], scale=scale2[:, kk:kk + 1])
            last.then_inc(S["xf_ok"], 1)

        def high_unit(i, n, b, m):
            u, w = 2 * n + m, width(b)
            act.wait_ge(wraw_in[u % 4], i * (16 * UNITS // 4) + 16 * (u // 4 + 1))
            need(act, "gu_ps", i * UNITS + (u - 1))
            act.activation(we_hi[:, m, :, 0:w], wraw[:, u % 4, :, 0:w], ACT.Copy).then_inc(S["hi_ok"], 1)

        def gate_unit(i, n, b):
            act.wait_ge(S["gu_ps"], i * UNITS + (2 * n + 1))
            need(act, "hid_ok", i * PAIR + n)
            act.activation(sil[:, 0:width(b)], bank[2 * (n % 2)][:, 0:width(b)], ACT.Silu).then_inc(S["sil_ok"], 1)

        def high_down(i, n):
            down_in(act, i, n)
            need(act, "d_ps", i * PAIR + n)
            act.activation(wd_hi[:, :, :], wdn[:, n % 2, 0:NS, :], ACT.Copy).then_inc(S["wdhi_ok"], 1)

        def hidden_out(i, n, b):
            act.wait_ge(S["hidT_ps"], i * PAIR + (n + 1))
            need(act, "d_ps", i * PAIR + (n - 1))
            ps, full = bank[4 + n % 2], width(b) // P
            tiles = lambda a, z: ps[:, a * P:z * P].rearrange("p (a b) -> p a b", b=P)
            act.activation(hidT_hi[:, n % 2, :, :], tiles(0, NS), ACT.Copy)
            last = act.activation(hidT[:, n % 2, 0:full - NS, :], tiles(NS, full), ACT.Copy)
            if width(b) % P:
                c = width(b) % P
                last = act.activation(hidT[0:c, n % 2, full - NS, :], ps[0:c, full * P:(full + 1) * P], ACT.Copy)
            last.then_inc(S["hidT_ok"], 1)

        def experts(i):
            for n, (ee, b) in enumerate(BLOCKS):
                before = not (isinstance(i, int) and i == 0 and n == 0)
                pb = BLOCKS[n - 1][1]
                if before:
                    high_unit(i, n, b, 0)
                    gate_unit(i, n - 1, pb)
                    high_unit(i, n, b, 1)
                    high_down(i, n - 1)
                if b in (3, 4):
                    token_out(i * 2 + (ee + 1), b - 3, bank[4 + (n - 2) % 2])
                if before:
                    hidden_out(i, n - 1, pb)

        for m in (0, 1):
            high_unit(0, 0, 0, m)
        for q in (0, 1):
            token_out(0, q, bank[4 + q])
        over_experts(act, experts)
        gate_unit(NE // 2, -1, NB - 1)
        high_down(NE // 2, -1)
        hidden_out(NE // 2, -1, NB - 1)

    def newton(v, y, var, tmp):
        v.tensor_tensor(tmp, y, y, ALU.mult)
        v.drain()
        v.tensor_tensor(tmp, tmp, var, ALU.mult)
        v.drain()
        v.tensor_scalar(tmp, tmp, -0.5, 1.5, ALU.mult, ALU.add)
        v.drain()
        return v.tensor_tensor(y, y, tmp, ALU.mult)

    def parts(v, src, dst, done):
        s = [src[:, 2 * n2:2 * n2 + 2, :].rearrange("p a b -> p (a b)") for n2 in range(4)]
        d = lambda i: dst[:, i, :]
        v.tensor_tensor(d(VA), s[0], s[2], ALU.add)
        v.tensor_tensor(d(VB), s[1], s[3], ALU.add)
        v.drain()
        v.tensor_tensor(d(V0), d(VA), d(VB), ALU.add).then_inc(S[done], 1)
        v.tensor_tensor(d(V4), d(VA), d(VB), ALU.subtract).then_inc(S[done], 1)
        v.tensor_tensor(d(R2), s[0], s[2], ALU.subtract)
        v.tensor_tensor(d(I2), s[1], s[3], ALU.subtract).then_inc(S[done], 1)
        v.drain()
        v.scalar_tensor_tensor(d(R1), d(I2), Q8, s[0], ALU.mult, ALU.add)
        v.scalar_tensor_tensor(d(I1), d(VB), Q8, s[2], ALU.mult, ALU.add).then_inc(S[done], 1)
        v.scalar_tensor_tensor(d(R3), d(I2), -Q8, s[0], ALU.mult, ALU.add)
        v.scalar_tensor_tensor(d(I3), d(VB), Q8, s[2], ALU.mult, ALU.subtract).then_inc(S[done], 1)

    @block.vector
    def _(v):
        v.memset(ones[:, :], 1.0).then_inc(S["ones_ok"], 1)
        v.wait_ge(S["cols_ps"], 1)
        v.tensor_copy(cols[:, :], bank[7][:, 0:132]).then_inc(S["cols_ok"], 1)
        MAGIC = 12582912.0
        TWO_PI_HI = 6.28125
        TWO_PI_LO = 2 * math.pi - TWO_PI_HI
        v.wait_ge(S["filt_in"], 7 * 16)
        v.wait_ge(S["silu_ok"], 1)
        v.tensor_copy(silu_b[:, :, :], silu_c[:, :, 0:1].to_broadcast([P, DK, P])).then_inc(S["silub_ok"], 1)
        for layer, b in ((0, 0), (1, 2)):
            v.wait_ge(S[("l1_ps", "l2_ps")[layer]], 1)
            if layer:
                v.wait_ge(S["sin_ok"], 1)
            for h in (0, 1):
                v.tensor_scalar(farg[:, h, :], bank[b + h][0:ORD, :], fcol[:, layer:layer + 1], fcol[:, 2:3],
                                ALU.add, ALU.mult)
            v.drain()
            v.tensor_scalar(fk[:, :, :], farg[:, :, :], 1.0 / (2 * math.pi), MAGIC, ALU.mult, ALU.add)
            v.drain()
            v.tensor_scalar(fk[:, :, :], fk[:, :, :], -MAGIC, None, ALU.add)
            v.drain()
            v.scalar_tensor_tensor(farg[:, :, :], fk[:, :, :], -TWO_PI_HI, farg[:, :, :], ALU.mult, ALU.add)
            v.drain()
            v.scalar_tensor_tensor(farg[:, :, :], fk[:, :, :], -TWO_PI_LO, farg[:, :, :], ALU.mult, ALU.add)
            v.drain()
            v.tensor_scalar(farg[:, :, :], farg[:, :, :], 3.1415925, -3.1415925, ALU.min, ALU.max
                            ).then_inc(S["sin_in"], 1)
        v.wait_ge(S["decay_in"], 16)
        for i in range(2 * TT):
            v.wait_ge(S["l3_ps"], i + 1)
            v.tensor_tensor((hfwd, hbwd)[i % 2][:, i // 2, :], bank[i % 4][:, :], decay[:, i // 2, :],
                            ALU.mult).then_inc(S["h_ok"], 1)
        v.drain()
        v.memset(hbwd[0:1, 0, :], 0.0).then_inc(S["h_ok"], 1)
        v.drain()
        v.tensor_tensor(hdif[:, :, :], hfwd[:, :, :], hbwd[:, :, :], ALU.subtract)
        v.wait_ge(S["habs_ok"], 1)
        v.drain()
        v.tensor_tensor(hfwd[:, :, :], hfwd[:, :, :], hbwd[:, :, :], ALU.add)
        w = TT * HYW
        v.tensor_tensor(habs[:, 0, :], habs[:, 0, :], habs[:, 1, :], ALU.add)
        while w > HYW:
            w //= 2
            v.drain()
            last = v.tensor_tensor(habs[:, 0, 0:w], habs[:, 0, 0:w], habs[:, 0, w:2 * w], ALU.add)
        last.then_inc(S["habs_sum"], 1)
        v.wait_ge(S["norm_ps"], 1)
        v.reciprocal(invn[:, :], bank[6][:, :]).then_inc(S["invn_ok"], 1)
        v.drain()
        parts(v, hfwd, vsum, "v_ok")
        parts(v, hdif, vdif, "v_ok")
        v.wait_ge(S["ssq_ok"], 1)
        v.drain()
        v.tensor_tensor(stat[:, 0, :], stat[:, 0, :], stat[:, 1, :], ALU.add)
        v.drain()
        v.tensor_scalar(stat[:, 1, :], stat[:, 0, :], 1.0 / DM, EPS, ALU.mult, ALU.add).then_inc(S["var_ok"], 1)
        v.wait_ge(S["sqrt_ok"], 1)
        v.reciprocal(rstd[:, :], stat[:, 2, :])
        v.drain()
        newton(v, rstd[:, :], stat[:, 1, :], stat[:, 0, :])
        v.wait_ge(S["mtr_ps"], 1)
        for b, c in ((0, 0), (32, 3 * DK)):
            for w in (0, 1):
                v.tensor_tensor(mod_t[:, c:c + 2 * DK, w], bank[7][:, b + w:b + 32:2],
                                cols[:, C_BM + c:C_BM + c + 2 * DK], ALU.add)
        v.drain()
        for w in (0, 1):
            v.scalar_tensor_tensor(scale1[:, :, w], mod_t[:, DK:2 * DK, w], 1.0, cols[:, C_G1:C_G1 + DK],
                                   ALU.add, ALU.mult)
        v.scalar_tensor_tensor(scale2[:, :], mod_t[:, 4 * DK:5 * DK, 0], 1.0, cols[:, C_G2:C_G2 + DK],
                               ALU.add, ALU.mult)
        v.sem_inc(S["xt_used"], 2)

        def scale_rows(i, h, par):
            v.wait_ge(xt_in[par], h * 16 + 16)
            v.tensor_scalar(xn[:, :], xt[:, par, :], rstd[:, bass.ds(i, 1)], None, ALU.mult).then_inc(S["xn_ok"], 1)
            v.drain()
            v.sem_inc(S["xt_used"], 1)

        v.wait_ge(S["bias_in"], 16)
        for i in range(2 * NCLS):
            v.wait_ge(S["kps"], i + 1)
            if i >= 4:
                v.wait_ge(kst[i % 4], 16 * (i // 4))
            v.tensor_tensor(kslot(i), bank[i % 4][:, :], invn[:, :], ALU.mult).then_inc(S["kmul"], 1)
            rows = slice(0, 1) if i == NCLS else slice(0, P)
            if i <= NCLS:
                v.drain()
                v.tensor_tensor(kslot(i)[rows], kslot(i)[rows], bias_b[rows, :], ALU.add).then_inc(S["kadd"], 1)
            if 4 <= i < 4 + DK:
                k = i - 4
                v.wait_ge(S["wqkvhi_ok"], k + 1)
                v.tensor_tensor(wqkv_lo[:, k, :], wqkv[:, k, :], wqkv_hi[:, k, :].bitcast(fp32), ALU.subtract
                                ).then_inc(S["wqkvlo_ok"], 1)
            if i == 4 + DK - 1:
                v.sem_inc(S["full_ok"], 1)
                scale_rows(0, 0, 0)

        v.drain()
        v.sem_inc(S["kv_ps"], 2)
        v.sem_inc(S["qn_ok"], 2)
        v.sem_inc(S["hT_in"], 64)

        def normalise(i, h, par):
            v.wait_ge(S["full_ok"], i + 2)
            if not (isinstance(i, int) and i == KT - 1):
                scale_rows(i + 1, h + par, 1 - par)
            v.wait_ge(S["kv_ps"], i + 1)
            v.wait_ge(S["hT_in"], i * 32 + 32)
            v.tensor_copy(hs_hi[:, par, :, :], hfull[:, :, :])
            v.drain()
            v.tensor_tensor(hs_lo[:, par, :, :], hfull[:, :, :], hs_hi[:, par, :, :].bitcast(fp32), ALU.subtract
                            ).then_inc(S["hs_ok"], 1)

        def low_wh_group(c, g):
            v.wait_ge(S["whhi_ok"], c * 3 + g + 1)
            v.tensor_tensor(wh_lo[:, g, :, :], wh[g][:, :, :], wh_hi[:, g, :, :].bitcast(fp32), ALU.subtract
                            ).then_inc(S["wh_ok"], 1)

        def head_norm(i, h, par):
            if isinstance(i, int) and i == KT - 1:
                v.sem_inc(S["wh_ok"], 3)
                v.sem_inc(S["evac_ok"], 6)
                v.sem_inc(S["conv_ok"], 3)
                v.sem_inc(S["uT_ok"], 1)
                v.sem_inc(S["proj_ps"], 6)
                low_wh_group(0, 0)
            g = slice(NQ, NH) if is_ctx(i) else slice(0, NH)
            v.wait_ge(S["sq_ok"], i + 1)
            v.tensor_reduce(qst[:, 3, g], qsq[:, g, :], AX.X, ALU.add)
            v.drain()
            v.tensor_scalar(qst[:, 0, g], qst[:, 3, g], 1.0 / HD, EPS, ALU.mult, ALU.add).then_inc(S["qvar_ok"], 1)
            v.wait_ge(S["qsd_ok"], i + 1)
            v.reciprocal(qst[:, 2, g], qst[:, 1, g])
            v.drain()
            newton(v, qst[:, 2, g], qst[:, 0, g], qst[:, 3, g])
            v.drain()
            need(v, "qk_ok", i)
            if not is_ctx(i):
                v.tensor_tensor(qn[:, 0:NQ, :], bank[2 + par][:, :].rearrange("p (a b) -> p a b", b=HD),
                                qst[:, 2, 0:NQ].unsqueeze(2).to_broadcast([P, NQ, HD]), ALU.mult)
            v.tensor_tensor(qn[:, NQ:NH, :], bank[4 + par][:, 0:QKW - QW].rearrange("p (a b) -> p a b", b=HD),
                            qst[:, 2, NQ:NH].unsqueeze(2).to_broadcast([P, NKV, HD]), ALU.mult
                            ).then_inc(S["qn_ok"], 1)

        over_tiles(v, normalise, head_norm)

        v.wait_ge(S["qk_ok"], KT)
        v.wait_ge(S["kv_ps"], KT + 2)
        v.wait_ge(S["hT_in"], 64 + 32 * TT)
        v.drain()
        v.memset(pad[:, :, 0:1], 0.0)
        v.memset(pad[:, :, SEQ + 1:SEQ + 2], 0.0)
        v.drain()

        def low_wh(c):
            for g in range(3):
                if not (isinstance(c, int) and c == 0 and g == 0):
                    low_wh_group(c, g)

        def convolve(c, ahead):
            for g in range(3):
                if g == 2 and isinstance(c, int) and c == HC - 1:
                    v.wait_ge(S["uT_ok"], HC + 1)
                    v.wait_ge(S["proj_ps"], 6 * HC + 6)
                    v.drain()
                    parts(v, uT, vu, "vu_ok")
                v.wait_ge(S["evac_ok"], c * 6 + 2 * g + 8)
                w = [cols[:, bass.ds(c + (C_CW + tap * 12 + GROUP[g] * HC), 1)] for tap in range(3)]
                b = cols[:, bass.ds(c + (C_CB + GROUP[g] * HC), 1)]
                if g == 1:
                    need(v, "uT_ps", c)
                dst = (vconv[:, :], gated[:, :], x2_all[:, bass.ds(c, 1), :].squeeze(1))[g]
                v.tensor_scalar(dst, pad[:, g, 1:SEQ + 1], w[1], b, ALU.mult, ALU.add)
                v.drain()
                v.scalar_tensor_tensor(dst, pad[:, g, 0:SEQ], w[0], dst, ALU.mult, ALU.add)
                v.drain()
                last = v.scalar_tensor_tensor(dst, pad[:, g, 2:SEQ + 2], w[2], dst, ALU.mult, ALU.add)
                last.then_inc(S["conv_ok"], 1)
                if g == 1:
                    v.drain()
                    v.tensor_tensor(gated[:, :], gated[:, :], vconv[:, :], ALU.mult).then_inc(S["u_ok"], 1)
                    ahead()
            v.drain()
            v.sem_inc(S["x2_ok"], 1)

        over_channels(v, low_wh, convolve)
        for i in range(NCLS):
            b = 2 * (i % 4)
            v.wait_ge(kin_in[i % 2], 32 * (i // 2 + 1))
            if i >= 2:
                v.wait_ge(S["y_ok"], i - 1)
            v.wait_ge(S["us_ps"], 2 * i + 2)
            kr, kn = kin[:, i % 2, 0, :], kin[:, i % 2, 1, :]
            for n, (u, k) in enumerate(((b, kr), (b + 1, kn), (b, kn), (b + 1, kr))):
                last = v.tensor_tensor(prod[:, i % 2, n, :], bank[u][:, :], k, ALU.mult)
            last.then_inc(S["prod_ok"], 1)
        v.wait_ge(S["kshi_ok"], 1)
        for w in (0, 1):
            last = v.tensor_tensor(ks_lo[:, :, :, w, :], qk_all[:, :, NQ:NH, :], ks_hi[:, :, :, w, :].bitcast(fp32),
                                   ALU.subtract)
        last.then_inc(S["kslo_ok"], 1)
        v.sem_inc(S["te_ok"], 2 * LAG)
        v.sem_inc(S["td_ok"], LAG)
        v.sem_inc(S["t_ps"], 3 * LAG)
        v.sem_inc(S["p_ok"], 2)

        def low_q(r):
            for hh in (0, 1):
                v.wait_ge(S["qshi_ok"], r * 2 + hh + 1)
                v.tensor_tensor(qs[:, hh, :, 1, :], qk_all[:, 0:TT, bass.ds(r + 4 * hh, 1), :].squeeze(2),
                                qs[:, hh, :, 0, :].bitcast(fp32), ALU.subtract).then_inc(S["qslo_ok"], 1)

        v.wait_ge(S["y_ok"], NCLS)
        for c in range(HC):
            if c == HC - 1:
                low_q(0)
            v.wait_ge(S["z_ok"], c + 1)
            zr = [zs[:, c % 2, z, 0:N1] for z in range(4)]
            zi = [zs[:, c % 2, z, N1:512] for z in range(4)]
            A, B, E, D, F, G, DF, SF = [ztmp[:, n, :] for n in range(8)]
            y = [ysum[:, n, :] for n in range(4)]
            for dst, p0, p1, op in ((A, zr[0], zi[0], ALU.add), (B, zr[0], zi[0], ALU.subtract),
                                    (E, zr[1], zr[3], ALU.add), (D, zr[1], zr[3], ALU.subtract),
                                    (F, zi[1], zi[3], ALU.add), (G, zi[3], zi[1], ALU.subtract)):
                v.tensor_tensor(dst, p0, p1, op)
            v.drain()
            for dst, p0, p1, op in ((y[0], A, zr[2], ALU.add), (y[2], A, zr[2], ALU.subtract),
                                    (y[1], B, zi[2], ALU.subtract), (y[3], B, zi[2], ALU.add),
                                    (DF, D, F, ALU.subtract), (SF, D, F, ALU.add)):
                v.tensor_tensor(dst, p0, p1, op)
            v.drain()
            v.tensor_tensor(y[0], y[0], E, ALU.add)
            v.tensor_tensor(y[2], y[2], G, ALU.add)
            v.scalar_tensor_tensor(y[1], DF, Q8, y[1], ALU.mult, ALU.add)
            v.scalar_tensor_tensor(y[3], SF, -Q8, y[3], ALU.mult, ALU.add)
            v.drain()
            v.tensor_tensor(mix_hy[:, c, :], ysum[:, :, :].rearrange("p a b -> p (a b)"), x2_all[:, c, :], ALU.mult
                            ).then_inc(S["mixhy_ok"], 1)

        v.drain()
        v.sem_inc(S["at_free"], 1)

        def maxima(r, kind):
            for s, rounds in enumerate(ROUNDS[kind]):
                if rounds and not (kind == "first" and s < LAG):
                    b, (a, z), k = (s - LAG) % STEPS, TROUND[2], thirds_done(kind, s)
                    v.wait_ge(S["t_ps"], r * RB + (k + 1))
                    v.tensor_copy(probT[:, b // 4 % 2, a:z, (b % 4) * P:(b % 4 + 1) * P],
                                  bank[6 + k % 2][:, 0:(z - a) * P].rearrange("p (a b) -> p a b", b=P)
                                  ).then_inc(S["td_ok"], 1)
                if kind != "tail":
                    v.wait_ge(S["s_ps"], r * STEPS + s + 1)
                    v.tensor_reduce(nmax[:, s % 4:s % 4 + 1], psum[:, SET * (s % 2):SET * (s % 2) + KT * P], AX.X,
                                    ALU.max, negate=True).then_inc(S["mx_ok"], 1)
                if not (kind == "first" and s == 0) and not (kind == "tail" and s > 0):
                    v.wait_ge(S["p_ok"], r * STEPS + s + 2)
                    v.reciprocal(prcp[:, (s - 1) % 4:(s - 1) % 4 + 1], psums[:, (s - 1) % 4:(s - 1) % 4 + 1]
                                 ).then_inc(S["rs_ok"], 1)
                if s == V_SLOT[1] or (s == V_SLOT[0] and kind != "first"):
                    pair, half = (r, 0) if s > 8 else (r - 1, 1)
                    v.wait_ge(S["pv_ps"], r * 2 + (s > 8))
                    v.tensor_copy(mix_at[:, bass.ds(pair, 1), half * 512:(half + 1) * 512].squeeze(1), bank[V_BANK][:, :]
                                  ).then_inc(S["pve_ok"], 1)
                if s == 9 and kind != "last":
                    low_q(r + 1)

        over_pairs(v, maxima)

        def low_mix(i, par):
            v.wait_ge(S["mshi_ok"], i + 1)
            v.tensor_tensor(ms_lo[:, par, 0:4, :], mix_at[:, :, bass.ts(i, P)], ms_hi[:, par, 0:4, :].bitcast(fp32),
                            ALU.subtract)
            v.tensor_tensor(ms_lo[:, par, 4:8, :], mix_hy[:, :, bass.ts(i, P)], ms_hi[:, par, 4:8, :].bitcast(fp32),
                            ALU.subtract).then_inc(S["ms_ok"], 1)

        def ahead_low(i, h, par):
            if not (isinstance(i, int) and i == TT - 1):
                low_mix(i + 1, 1 - par)

        def residual_and_route(i, h, par):
            c = lambda n: st2[:, n, par:par + 1]
            v.wait_ge(xr_in[par], h * 16 + 16)
            v.wait_ge(S["o_ps"], i + 1)
            v.wait_ge(xst[par], h * 32 + 32)
            for half in (0, 1):
                v.tensor_tensor(gmix[:, half * 512:(half + 1) * 512], bank[2 * par + half][:, :],
                                gate_b[:, 0, half * 512:(half + 1) * 512], ALU.mult)
            v.drain()
            v.tensor_tensor(x1[:, par, :], gmix[:, :], xr[:, par, :], ALU.add).then_inc(S["x1_ok"], 1)
            v.wait_ge(S["ssq2_ok"], i + 1)
            v.tensor_scalar(c(1), c(0), 1.0 / DM, EPS, ALU.mult, ALU.add).then_inc(S["var2_ok"], 1)
            v.wait_ge(S["sd2_ok"], i + 1)
            v.reciprocal(c(3), c(2))
            v.drain()
            newton(v, c(3), c(1), c(4))
            v.drain()
            need(v, "x2T_ps", i)
            v.tensor_scalar(xn2[:, par, :], x1[:, par, :], c(3), None, ALU.mult).then_inc(S["xn2_ok"], 1)

        for par in (0, 1):
            v.sem_inc(xst[par], 32)
        low_mix(0, 0)
        for k in range(DK):
            v.wait_ge(S["wohi_ok"], k + 1)
            v.tensor_tensor(wo_lo[:, k, :], wo[:, k % 4, :], wo_hi[:, k, :].bitcast(fp32), ALU.subtract
                            ).then_inc(S["wo_ok"], 1)
        over_out(v, ahead_low, residual_and_route)
        nmx, rsum = rst[:, 0, :], rst[:, 1, :]
        wide = lambda a: a.unsqueeze(2).to_broadcast([P, TT, NE])
        v.wait_ge(S["lg_ok"], TT)
        v.tensor_reduce(nmx, logit[:, :, :], AX.X, ALU.max, negate=True)
        v.drain()
        v.tensor_tensor(logit[:, :, :], logit[:, :, :], wide(nmx), ALU.add).then_inc(S["rmx_ok"], 1)
        v.wait_ge(S["rexp_ok"], 1)
        v.tensor_reduce(rsum, logit[:, :, :], AX.X, ALU.add)
        v.drain()
        v.reciprocal(rsum, rsum)
        v.drain()
        v.tensor_tensor(aff_t[:, :, :, :].rearrange("p q h e -> p h q e"),
                        logit[:, :, :].rearrange("p (h q) e -> p h q e", h=2),
                        wide(rsum).rearrange("p (h q) e -> p h q e", h=2), ALU.mult).then_inc(S["aff_ok"], 1)
        v.wait_ge(S["affT_ok"], 1)
        for r in range(CAP // 8):
            src, dst = aff[:, r % 2, :], aff[:, 1 - r % 2, :]
            best = top_v[:, 8 * r:8 * r + 8]
            v.max(best, src)
            v.drain()
            v.max_index(top_i[:, 8 * r:8 * r + 8], best, src)
            if r < CAP // 8 - 1:
                v.match_replace(dst, best, src, -1.0)
            v.drain()
        v.tensor_copy(top_f[:, :], top_i[:, :]).then_inc(S["top_ok"], 1)
        v.wait_ge(S["tops_ps"], 1)
        v.tensor_copy(cand[:, :, :, :].rearrange("p a b c -> p (a b c)"), bank[6][:, 0:4 * NE]).then_inc(S["top_ok"], 1)
        v.wait_ge(S["tops_ps"], 2)
        turned = bank[7][:, 0:4 * NE].rearrange("p (a b c) -> p a b c", a=2, b=2)
        first, other, token = [pick[:, n, :] for n in range(3)]
        v.tensor_tensor(slot_g[:, :], cand[:, 0, 0, :], turned[:, 0, 1, :], ALU.max)
        v.tensor_tensor(first, cand[:, 0, 0, :], turned[:, 0, 1, :], ALU.is_ge)
        v.tensor_scalar(other, turned[:, 1, 1, :], float(SEQ // 2), None, ALU.add)
        v.drain()
        v.tensor_tensor(token, cand[:, 1, 0, :], other, ALU.subtract)
        v.drain()
        v.tensor_tensor(token, token, first, ALU.mult)
        v.drain()
        v.tensor_tensor(token, token, other, ALU.add)
        v.drain()
        v.tensor_copy(slot_i[:, NE:NE + 2], token[:, 0:2])
        v.tensor_copy(slot_i[:, 0:NE], token).then_inc(S["slots_ok"], 1)
        def split_tokens(e, slot):
            v.wait_ge(S["xf_ok"], e * 2 + 2)
            v.tensor_copy(xe_hi[:, slot, :, :], xf[:, :, :])
            v.drain()
            v.tensor_tensor(xe_lo[:, slot, :, :], xf[:, :, :], xe_hi[:, slot, :, :].bitcast(fp32), ALU.subtract
                            ).then_inc(S["xe_ok"], 1)

        def low_unit(i, n, b, m):
            u, w = 2 * n + m, width(b)
            v.wait_ge(S["hi_ok"], i * UNITS + (u + 1))
            v.tensor_tensor(we_lo[:, m, :, 0:w], wraw[:, u % 4, :, 0:w], we_hi[:, m, :, 0:w].bitcast(fp32),
                            ALU.subtract).then_inc(S["lo_ok"], 1)

        def hidden(i, n, b):
            w = width(b)
            v.wait_ge(S["sil_ok"], i * PAIR + (n + 1))
            v.wait_ge(S["gu_ps"], i * UNITS + (2 * n + 2))
            need(v, "hidT_ps", i * PAIR + (n - 1))
            v.tensor_tensor(hid[:, n % 2, 0:w], sil[:, 0:w], bank[2 * (n % 2) + 1][:, 0:w], ALU.mult
                            ).then_inc(S["hid_ok"], 1)

        def low_down(i, n):
            v.wait_ge(S["wdhi_ok"], i * PAIR + (n + 1))
            v.tensor_tensor(wd_lo[:, :, :], wdn[:, n % 2, 0:NS, :], wd_hi[:, :, :].bitcast(fp32), ALU.subtract
                            ).then_inc(S["wdlo_ok"], 1)
            v.wait_ge(S["hidT_ok"], i * PAIR + (n + 1))
            v.tensor_tensor(hidT_lo[:, n % 2, :, :], bank[4 + n % 2][:, 0:NS * P].rearrange("p (a b) -> p a b", b=P),
                            hidT_hi[:, n % 2, :, :].bitcast(fp32), ALU.subtract).then_inc(S["hlo_ok"], 1)

        def result(e):
            v.wait_ge(S["d_ps"], e * NB + NB)
            need(v, "scat", e * 16)
            for half in (0, 1):
                cs = slice(half * 512, (half + 1) * 512)
                last = v.scalar_tensor_tensor(yb[:, cs], bank[6 + half][:, :], slot_g[:, bass.ds(e, 1)],
                                              gate_b[:, 1, cs], ALU.mult, ALU.mult)
            last.then_inc(S["ye_ok"], 1)

        def experts(i):
            for n, (ee, b) in enumerate(BLOCKS):
                if not (isinstance(i, int) and i == 0 and n == 0):
                    low_unit(i, n, b, 0)
                    hidden(i, n - 1, BLOCKS[n - 1][1])
                    low_unit(i, n, b, 1)
                    low_down(i, n - 1)
                if b == 1 and not (isinstance(i, int) and i == 0 and ee == 0):
                    result(i * 2 + (ee - 1))
                if b == 5:
                    split_tokens(i * 2 + (ee + 1), 1 - ee)

        for m in (0, 1):
            low_unit(0, 0, 0, m)
        split_tokens(0, 0)
        over_experts(v, experts)
        hidden(NE // 2, -1, NB - 1)
        low_down(NE // 2, -1)
        result(NE - 1)

    ctx.close()


_DRAWN = """x c ctx c_ctx w_mod b_mod norm1_g norm2_g w_in w_out q_norm_g k_norm_g conv_w conv_b filt_w1 filt_b1
    filt_w2 filt_b2 filt_w3 filt_freq hyena_bias w_router w_gate w_up w_down""".split()


def kernel(**inputs):
    import numpy as np
    import concourse.bacc as bacc
    from concourse.bass_utils import run_bass_kernel_spmd as run

    nc = bacc.Bacc("TRN2", target_bir_lowering=False, num_devices=1)
    arrays, aps = {}, {}
    given = {n: np.ascontiguousarray(inputs[n]) for n in _DRAWN}
    given.update(constants())
    for name, a in given.items():
        arrays["in_" + name] = a
        aps[name] = nc.dram_tensor("in_" + name, a.shape, mybir.dt.from_np(a.dtype), kind="ExternalInput").ap()
    out = nc.dram_tensor("out", [1, SEQ, DM], mybir.dt.float32, kind="ExternalOutput").ap()
    build(nc, aps, out)
    r = run(nc, [arrays], core_ids=[0])
    return r.results[0]["out"]
```
